# Optimizing a Trainium2 kernel written in Bass

```python
import math
import jax, jax.numpy as jnp
from jax import lax
import numpy as np

D_MODEL = 1024
BATCH = 1
SEQ = 512
DEPTH = 1

GRID_W = 64
HEAD_DIM = 64
N_HEADS_DN = D_MODEL // (2 * HEAD_DIM)
N_HEADS_NA = D_MODEL // (2 * HEAD_DIM)
DN_WIDTH = N_HEADS_DN * HEAD_DIM
NA_WIDTH = N_HEADS_NA * HEAD_DIM
MIX_WIDTH = DN_WIDTH + NA_WIDTH
DN_CONV = 5
DN_CHUNK = 64
NA_WIN_H = 8
NA_WIN_W = 16
N_GROUPS = 4
EXPERTS_PER_GROUP = 8
N_EXPERTS = N_GROUPS * EXPERTS_PER_GROUP
TOP_K_EXPERT = 2
D_EXPERT = 512
EPS = 1e-6
IN_SPLITS = (DN_WIDTH, DN_WIDTH, DN_WIDTH, DN_WIDTH, N_HEADS_DN, N_HEADS_DN, N_HEADS_DN, N_HEADS_DN, NA_WIDTH, NA_WIDTH, NA_WIDTH)
IN_WIDTH = 4 * DN_WIDTH + 4 * N_HEADS_DN + 3 * NA_WIDTH

kernel_name = "hybrid_deltanet_natten_hmoe_block"

def rmsnorm(x, w):
    x32 = x.astype(jnp.float32)
    y = x32 * lax.rsqrt(jnp.mean(x32 * x32, axis=-1, keepdims=True) + EPS)
    return (y * w.astype(jnp.float32)).astype(x.dtype)

def l2norm(x):
    x32 = x.astype(jnp.float32)
    return x32 * lax.rsqrt(jnp.sum(x32 * x32, axis=-1, keepdims=True) + EPS)

def centred_depthwise_conv(x, w):
    k_w, ch = w.shape
    pad = (k_w - 1) // 2
    return lax.conv_general_dilated(x, w[:, None, :].astype(x.dtype), window_strides=(1,), padding=[(pad, pad)],
                                    dimension_numbers=("NWC", "WIO", "NWC"), feature_group_count=ch)

def gated_delta_rule_chunked(q, k, v, g, beta):
    B, H, S, dk = q.shape
    dv = v.shape[-1]
    n = S // DN_CHUNK

    def chunks(t):
        return t.reshape(B, H, n, DN_CHUNK, *t.shape[3:])

    q = chunks(q * dk ** -0.5)
    k, v, g, beta = chunks(k), chunks(v), chunks(g), chunks(beta)
    g_cum = jnp.cumsum(g, axis=-1)
    incl = jnp.tril(jnp.ones((DN_CHUNK, DN_CHUNK), dtype=bool))
    strict = jnp.tril(jnp.ones((DN_CHUNK, DN_CHUNK), dtype=bool), k=-1)
    diff = g_cum[..., :, None] - g_cum[..., None, :]
    decay = jnp.where(incl, jnp.exp(jnp.where(incl, diff, 0.0)), 0.0)
    k_beta = k * beta[..., None]
    m = jnp.where(strict, jnp.einsum("bhnid,bhnjd->bhnij", k_beta, k) * decay, 0.0)
    eye = jnp.eye(DN_CHUNK, dtype=q.dtype)
    t_inv = lax.linalg.triangular_solve(m + eye, jnp.broadcast_to(eye, m.shape), left_side=True,
                                        lower=True, unit_diagonal=True)
    u = jnp.einsum("bhnij,bhnje->bhnie", t_inv, v * beta[..., None])
    w = jnp.einsum("bhnij,bhnjd->bhnid", t_inv, k_beta * jnp.exp(g_cum)[..., None])
    attn = jnp.where(incl, jnp.einsum("bhnid,bhnjd->bhnij", q, k) * decay, 0.0)
    q_dec = q * jnp.exp(g_cum)[..., None]
    g_last = g_cum[..., -1]
    k_tail = k * jnp.exp(g_last[..., None] - g_cum)[..., None]

    def step(state, xs):
        q_c, k_c, u_c, w_c, a_c, gl_c = xs
        v_new = u_c - jnp.einsum("bhcd,bhde->bhce", w_c, state)
        o_c = jnp.einsum("bhcd,bhde->bhce", q_c, state) + jnp.einsum("bhij,bhje->bhie", a_c, v_new)
        state = state * jnp.exp(gl_c)[..., None, None] + jnp.einsum("bhcd,bhce->bhde", k_c, v_new)
        return state, o_c

    xs = (jnp.moveaxis(q_dec, 2, 0), jnp.moveaxis(k_tail, 2, 0), jnp.moveaxis(u, 2, 0),
          jnp.moveaxis(w, 2, 0), jnp.moveaxis(attn, 2, 0), jnp.moveaxis(g_last, 2, 0))
    state0 = jnp.zeros((B, H, dk, dv), q.dtype)
    _, o = lax.scan(step, state0, xs)
    return jnp.moveaxis(o, 0, 2).reshape(B, H, S, dv)

def neighbourhood_attention(q, k, v, rpb):
    B, S, H, d = q.shape
    rows = S // GRID_W
    win_h = min(NA_WIN_H, rows)
    r = np.arange(rows)
    r0 = np.clip(r - win_h // 2, 0, rows - win_h)
    key_rows = r0[:, None] + np.arange(win_h)[None, :]
    cc = np.arange(GRID_W)
    c0 = np.clip(cc - NA_WIN_W // 2, 0, GRID_W - NA_WIN_W)
    key_cols = c0[:, None] + np.arange(NA_WIN_W)[None, :]
    row_off = key_rows - r[:, None] + NA_WIN_H - 1
    col_off = key_cols - cc[:, None] + NA_WIN_W - 1
    bias = rpb[:, row_off[:, :, None, None], col_off[None, None, :, :]]
    bias = bias.transpose(1, 0, 3, 2, 4)
    qg = (q * d ** -0.5).reshape(B, rows, GRID_W, H, d).transpose(1, 0, 2, 3, 4)
    kg = k.reshape(B, rows, GRID_W, H, d)
    vg = v.reshape(B, rows, GRID_W, H, d)

    def row_attend(xs):
        q_r, rows_i, bias_r = xs
        k_nb = kg[:, rows_i][:, :, key_cols]
        v_nb = vg[:, rows_i][:, :, key_cols]
        s = jnp.einsum("bqhd,brqwhd->bhqrw", q_r, k_nb).astype(jnp.float32) + bias_r[None].astype(jnp.float32)
        p = jax.nn.softmax(s.reshape(B, H, GRID_W, -1), axis=-1).reshape(s.shape)
        return jnp.einsum("bhqrw,brqwhd->bqhd", p.astype(v.dtype), v_nb)

    o = lax.map(row_attend, (qg, jnp.asarray(key_rows), bias))
    return o.transpose(1, 0, 2, 3, 4).reshape(B, S, H * d)

def token_mixer(h, w_in, w_conv_dn, a_log_dn, dt_bias_dn, g_onorm_dn, rpb_na, w_out):
    B, S, _ = h.shape
    proj = h @ w_in
    qkv_dn = jax.nn.silu(centred_depthwise_conv(proj[..., :3 * DN_WIDTH], w_conv_dn))
    q_dn, k_dn, v_dn = jnp.split(qkv_dn, 3, axis=-1)
    _, _, _, z_dn, a_f, a_b, b_f, b_b, q_na, k_na, v_na = jnp.split(proj, np.cumsum(IN_SPLITS)[:-1].tolist(), axis=-1)

    def heads(t):
        return t.reshape(B, S, -1, HEAD_DIM).transpose(0, 2, 1, 3)

    qa, ka = l2norm(heads(q_dn)), l2norm(heads(k_dn))
    va = heads(v_dn).astype(jnp.float32)

    def log_decay(a, i):
        a32 = a.astype(jnp.float32).transpose(0, 2, 1)
        return -jnp.exp(a_log_dn[i].astype(jnp.float32))[None, :, None] * jax.nn.softplus(
            a32 + dt_bias_dn[i].astype(jnp.float32)[None, :, None])

    g_f, g_b = log_decay(a_f, 0), log_decay(a_b, 1)
    beta_f = jax.nn.sigmoid(b_f.astype(jnp.float32).transpose(0, 2, 1))
    beta_b = jax.nn.sigmoid(b_b.astype(jnp.float32).transpose(0, 2, 1))
    o_f = gated_delta_rule_chunked(qa, ka, va, g_f, beta_f)

    def flip(t):
        return jnp.flip(t, axis=2)

    o_b = flip(gated_delta_rule_chunked(flip(qa), flip(ka), flip(va), flip(g_b), flip(beta_b)))
    o_dn = (o_f + o_b).transpose(0, 2, 1, 3)
    o_dn = rmsnorm(o_dn, g_onorm_dn) * jax.nn.silu(z_dn.reshape(B, S, N_HEADS_DN, HEAD_DIM).astype(jnp.float32))
    o_dn = o_dn.reshape(B, S, DN_WIDTH).astype(h.dtype)

    o_na = neighbourhood_attention(q_na.reshape(B, S, N_HEADS_NA, HEAD_DIM), k_na.reshape(B, S, N_HEADS_NA, HEAD_DIM),
                                   v_na.reshape(B, S, N_HEADS_NA, HEAD_DIM), rpb_na)
    return jnp.concatenate([o_dn, o_na.astype(h.dtype)], axis=-1) @ w_out

def hierarchical_moe(h, w_group, b_group, w_expert, b_expert, w_gate, w_up, w_down):
    B, S, D = h.shape
    t = h.reshape(B * S, D)
    group_p = jax.nn.softmax((t @ w_group + b_group).astype(jnp.float32), axis=-1)
    gp_top, g_idx = lax.top_k(group_p, 1)
    exp_logits = (t @ w_expert + b_expert).astype(jnp.float32).reshape(-1, N_GROUPS, EXPERTS_PER_GROUP)
    in_group = jnp.einsum("tg,tge->te", jax.nn.one_hot(g_idx[:, 0], N_GROUPS, dtype=jnp.float32), exp_logits)
    ep_top, e_idx = lax.top_k(jax.nn.softmax(in_group, axis=-1), TOP_K_EXPERT)
    weights = gp_top * ep_top / jnp.sum(ep_top, axis=-1, keepdims=True)
    expert_id = g_idx * EXPERTS_PER_GROUP + e_idx
    combine = jnp.einsum("tk,tke->te", weights, jax.nn.one_hot(expert_id, N_EXPERTS, dtype=jnp.float32))
    y = jnp.zeros(t.shape, jnp.float32)
    for e in range(N_EXPERTS):
        he = jax.nn.silu(t @ w_gate[e]) * (t @ w_up[e])
        y = y + combine[:, e:e + 1] * (he @ w_down[e]).astype(jnp.float32)
    return y.astype(h.dtype).reshape(B, S, D)

def setup_inputs(seed: int = 0) -> dict:
    key = jax.random.key(seed)
    ks = jax.random.split(key, 24)
    f32 = jnp.float32

    def nrm(k, shape, scale):
        return jax.random.normal(k, shape, f32) * scale

    def gain(k, shape):
        return 1.0 + 0.05 * jax.random.normal(k, shape, f32)

    dt = jnp.exp(jax.random.uniform(ks[9], (DEPTH, 2, N_HEADS_DN), f32, math.log(1e-3), math.log(1e-1)))
    return {
        "x": nrm(ks[0], (BATCH, SEQ, D_MODEL), 1.0),
        "c": nrm(ks[1], (BATCH, D_MODEL), 1.0),
        "w_ada": nrm(ks[2], (DEPTH, D_MODEL, 6 * D_MODEL), 0.5 * D_MODEL ** -0.5),
        "b_ada": nrm(ks[3], (DEPTH, 6 * D_MODEL), 0.02),
        "g_pre_mix": gain(ks[4], (DEPTH, D_MODEL)),
        "g_post_mix": gain(ks[5], (DEPTH, D_MODEL)),
        "w_in": nrm(ks[6], (DEPTH, D_MODEL, IN_WIDTH), D_MODEL ** -0.5),
        "w_conv_dn": nrm(ks[7], (DEPTH, DN_CONV, 3 * DN_WIDTH), DN_CONV ** -0.5),
        "a_log_dn": jnp.log(jax.random.uniform(ks[8], (DEPTH, 2, N_HEADS_DN), f32, 1.0, 16.0)),
        "dt_bias_dn": dt + jnp.log(-jnp.expm1(-dt)),
        "g_onorm_dn": gain(ks[10], (DEPTH, HEAD_DIM)),
        "rpb_na": nrm(ks[11], (DEPTH, N_HEADS_NA, 2 * NA_WIN_H - 1, 2 * NA_WIN_W - 1), 0.1),
        "w_out": nrm(ks[12], (DEPTH, MIX_WIDTH, D_MODEL), MIX_WIDTH ** -0.5),
        "g_pre_ffn": gain(ks[13], (DEPTH, D_MODEL)),
        "g_post_ffn": gain(ks[14], (DEPTH, D_MODEL)),
        "w_group": nrm(ks[15], (DEPTH, D_MODEL, N_GROUPS), D_MODEL ** -0.5),
        "b_group": nrm(ks[16], (DEPTH, N_GROUPS), 0.01),
        "w_expert": nrm(ks[17], (DEPTH, D_MODEL, N_EXPERTS), D_MODEL ** -0.5),
        "b_expert": nrm(ks[18], (DEPTH, N_EXPERTS), 0.01),
        "w_gate": nrm(ks[19], (DEPTH, N_EXPERTS, D_MODEL, D_EXPERT), D_MODEL ** -0.5),
        "w_up": nrm(ks[20], (DEPTH, N_EXPERTS, D_MODEL, D_EXPERT), D_MODEL ** -0.5),
        "w_down": nrm(ks[21], (DEPTH, N_EXPERTS, D_EXPERT, D_MODEL), D_EXPERT ** -0.5),
    }

def reference(x, c, w_ada, b_ada, g_pre_mix, g_post_mix, w_in, w_conv_dn, a_log_dn, dt_bias_dn, g_onorm_dn,
              rpb_na, w_out, g_pre_ffn, g_post_ffn, w_group, b_group, w_expert, b_expert, w_gate, w_up, w_down):
    cond = jax.nn.silu(c)
    for l in range(DEPTH):
        ada = cond @ w_ada[l] + b_ada[l]
        sh1, sc1, gt1, sh2, sc2, gt2 = jnp.split(ada[:, None, :], 6, axis=-1)
        h = rmsnorm(x, g_pre_mix[l]) * (1.0 + sc1) + sh1
        y = token_mixer(h, w_in[l], w_conv_dn[l], a_log_dn[l], dt_bias_dn[l], g_onorm_dn[l], rpb_na[l], w_out[l])
        x = x + gt1 * rmsnorm(y, g_post_mix[l])
        h = rmsnorm(x, g_pre_ffn[l]) * (1.0 + sc2) + sh2
        y = hierarchical_moe(h, w_group[l], b_group[l], w_expert[l], b_expert[l], w_gate[l], w_up[l], w_down[l])
        x = x + gt2 * rmsnorm(y, g_post_ffn[l])
    return x


_drawn_inputs = setup_inputs


def setup_inputs(seed=0):
    import zlib

    import numpy as np

    out = dict(_drawn_inputs(seed))
    spreads = {}
    factors = {'g_post_ffn': 4.337, 'b_group': 3.214, 'b_expert': 4.559}
    for name, (base, spread) in spreads.items():
        noise = np.random.default_rng([zlib.crc32(name.encode()), seed]).standard_normal(out[name].shape)
        drawn = base * np.exp(spread * noise) if base else spread * noise
        out[name] = __import__('jax').numpy.asarray(drawn.astype(out[name].dtype))
    for name, factor in factors.items():
        out[name] = (out[name] * factor).astype(out[name].dtype)
    return out
```

```python
from contextlib import ExitStack

import numpy as np

import concourse.bass as bass
from concourse import mybir

F32 = mybir.dt.float32
I32 = mybir.dt.int32
U32 = mybir.dt.uint32
ALU = mybir.AluOpType
ACT = mybir.ActivationFunctionType
AX = mybir.AxisListType

P = 128
T = 512
D = 1024
TT = T // P
KC = D // P
HD = 64
NH = 8
HW = NH * HD
FC = HW // P
CH = 64
STEPS = T // CH
CONV = 5
PAD = CONV // 2
GRID_W, ROWS, WIN = 64, 8, 16
KB = 8
WC = 32
QB = 48
NG, EG, NE = 4, 8, 32
DE = 512
SL = 64
LEVELS = 6
EPS = 1e-6
NEG = -1e30

C_BADA, C_G1, C_P1, C_G2, C_P2, C_C = 0, 48, 56, 64, 72, 80
C_CONV, C_ONORM, C_ALOG, C_DT, C_RB = 88, 148, 149, 157, 165
NCOL = C_RB + NG + NE


def constants():
    i = np.arange(P)
    ci = i % CH
    half = i // CH
    same = half[:, None] == half[None, :]
    fwd = (half == 0)[:, None]
    r, c = ci[:, None], ci[None, :]
    j = np.arange(CH)[None, :]
    out = {
        "ident": np.eye(P),
        "fold": np.concatenate([np.eye(CH)] * 2),
        "after": same * np.where(fwd, r > c, r < c),
        "upto": same * np.where(fwd, r <= c, r >= c),
        "uptoc": np.where(half[:, None] == 0, r <= j, r >= j),
        "halves": same * 1.0,
    }
    levels = []
    for s in range(LEVELS):
        b = 2 ** s
        pair = (r // (2 * b)) == (j // (2 * b))
        f = pair & ((j // b) % 2 == 1) & ((r // b) % 2 == 0)
        g = pair & ((j // b) % 2 == 0) & ((r // b) % 2 == 1)
        levels.append(np.where(half[:, None] == 0, f, g))
    out["levels"] = np.stack(levels, 1).reshape(P, LEVELS * CH)
    q = i % WIN
    masks = []
    for delta, base in ((0, 0), (-8, 16), (-16, 48)):
        col = base + q
        c0 = np.clip(col - WIN // 2, 0, GRID_W - WIN)
        k = base + delta + np.arange(WC)
        ok = (k[None, :] >= c0[:, None]) & (k[None, :] < c0[:, None] + WIN)
        masks.append(np.where(ok, 0.0, NEG))
    out["window"] = np.stack(masks, 1).reshape(P, 3 * WC)
    out["slots"] = np.broadcast_to(np.arange(T)[None, :], (P, T))
    out["experts"] = np.broadcast_to(np.arange(NE)[None, :], (P, NE))
    out["before"] = (i[:, None] < i[None, :]) * 1.0
    out["ones"] = np.ones((P, P))
    out["tiles"] = np.broadcast_to(np.arange(1, T // SL)[None, :] * SL, (P, T // SL - 1))
    return {k: np.ascontiguousarray(v, dtype=np.float32) for k, v in out.items()}


CONST = {}
_at = 0
for _k, _w in (("ident", P), ("fold", CH), ("after", P), ("upto", P), ("uptoc", CH), ("halves", P),
               ("levels", LEVELS * CH), ("window", 3 * WC), ("slots", T), ("experts", NE), 
               ("before", P), ("ones", P), ("tiles", T // SL - 1)):
    CONST[_k] = (_at, _w)
    _at += _w
NCONST = _at

SLOT = 4096
NSLOT = 6
M_HT = NSLOT * SLOT
M_QKV = M_HT + KC * T
M_Z = M_QKV + 3 * FC * T
M_MIX = M_Z + FC * T
M_NA = M_MIX + 2 * FC * T
M_C = M_NA + 3 * FC * T
M_COL = M_C + NCONST
M_WAB = M_COL + NCOL
M_MISC = M_WAB + KC * (NG + NE)
MEM = M_MISC + 2200


class Kernel:

    def __init__(self, nc, ctx, dram):
        self.nc, self.ctx, self.dram = nc, ctx, dram
        self.mem = ctx.enter_context(nc.sbuf_tensor("mem", [P, MEM], F32))
        self.banks = [ctx.enter_context(nc.psum_tensor(f"bank{i}", [P, 512], F32)) for i in range(8)]
        self.misc_at = M_MISC
        self.local = []
        self.stage = "all"
        self.mod = self.misc(48)
        self.g = self.misc(STEPS, NH)
        self.beta = self.misc(STEPS, NH)
        self.s_const = self.sem("s_const")
        self.s_cols = self.sem("s_cols")
        self.s_bias = self.sem("s_bias")
        self.s_expert = [[self.sem(f"s_{w}{j}") for w in ("gate", "up", "down")] for j in range(2)]
        self.free_misc = self.misc_at
        self.local = []

    def sem(self, name):
        s = self.nc.alloc_semaphore(name=f"{self.stage}_{name}")
        self.local.append(s)
        return s

    def end_stage(self):
        self.nc.clear_and_free_semaphores(self.local)
        self.nc.all_engine_barrier()
        self.local = []

    def view(self, at, *shape):
        n = int(np.prod(shape))
        v = self.mem[:, at:at + n]
        if len(shape) == 2:
            return v.rearrange("p (a b) -> p a b", b=shape[1])
        if len(shape) == 3:
            return v.rearrange("p (a b c) -> p a b c", b=shape[1], c=shape[2])
        if len(shape) == 4:
            return v.rearrange("p (a b c d) -> p a b c d", b=shape[1], c=shape[2], d=shape[3])
        return v

    def misc(self, *shape):
        at = self.misc_at
        self.misc_at += int(np.prod(shape))
        assert self.misc_at <= MEM
        return self.view(at, *shape)

    def const(self, name):
        at, w = CONST[name]
        return self.mem[:, M_C + at:M_C + at + w]

    def col(self, at, n=1):
        return self.mem[:, M_COL + at:M_COL + at + n]


ITEMS = [("ada", 0), ("ada", 1), ("ada", 2), ("ada", 3), ("in", 0), ("ada", 4), ("in", 1), ("ada", 5), ("in", 2),
         ("ada", 6), ("in", 3), ("ada", 7), ("in", 4), ("ada", 8), ("in", 5), ("ada", 9), ("in", 6), ("ada", 10),
         ("ada", 11)]
IN_AT = [0, HW, 2 * HW, 3 * HW, 4 * HW + 4 * NH, 5 * HW + 4 * NH, 6 * HW + 4 * NH]


def items_done(eng, k, n):
    ada = sum(kind == "ada" for kind, _ in ITEMS[:n])
    if ITEMS[n - 1][0] == "ada":
        eng.wait_ge(k.s_ada, ada)
    else:
        eng.wait_ge(k.s_tile, FC * (n - ada))


def project(k):
    nc, dram = k.nc, k.dram
    hT = k.view(M_HT, KC, T)
    qkv = k.view(M_QKV, 3 * FC, T)
    zT = k.view(M_Z, FC, T)
    na = k.view(M_NA, 3 * FC, T)
    x_sb = k.view(M_NA, TT, D)
    padded = [k.mem[:, M_MIX + i * 520:M_MIX + i * 520 + T + 2 * PAD] for i in range(2)]
    conv = [k.mem[:, M_MIX + 1040 + i * T:M_MIX + 1040 + (i + 1) * T] for i in range(2)]
    square = [k.mem[:, M_MIX + 2064 + i * T:M_MIX + 2064 + (i + 1) * T] for i in range(2)]
    inv = k.mem[:, M_MIX + 3088:M_MIX + 3088 + T]
    w_ab = k.view(M_WAB, KC, 4 * NH)
    junk = k.mem[:, M_QKV:M_QKV + D]
    ident = k.const("ident")
    amod, cond, stat, rstd = k.misc(KC), k.misc(KC), k.misc(TT), k.misc(TT)
    ga, gabs, gb = (k.misc(STEPS * NH).rearrange("p (s h) -> p s h", h=NH) for _ in range(3))
    expa = k.misc(NH)

    s_x = k.sem("s_x")
    s_ab_w = k.sem("s_ab_w")
    s_slot = [k.sem(f"s_slot{i}") for i in range(NSLOT)]
    k.s_ada = k.sem("s_ada")
    k.s_tile = k.sem("s_tile")
    s_cond = k.sem("s_cond")
    s_mod = k.sem("s_mod")
    s_stat = k.sem("s_stat")
    s_rstd = k.sem("s_rstd")
    s_xn = k.sem("s_xn")
    s_xT = k.sem("s_xT")
    s_hT = k.sem("s_hT")
    s_evac = k.sem("s_evac")
    s_evacv = k.sem("s_evacv")
    s_pad = k.sem("s_pad")
    s_tap = k.sem("s_tap")
    s_silu = k.sem("s_silu")
    s_sq = k.sem("s_sq")
    s_ss = k.sem("s_ss")
    s_inv = k.sem("s_inv")
    s_root = k.sem("s_root")
    k.s_norm = k.sem("s_norm")
    s_ab = k.sem("s_ab")
    s_gate = k.sem("s_gate")
    s_gact = k.sem("s_gact")

    NT = 7 * FC
    NDN = 3 * FC
    psA = [k.banks[0], k.banks[1]]
    RING = 4
    psP = k.banks[2:6]
    psS = k.banks[6]
    psG = k.banks[7]

    by_act = [f < 20 for f in range(NT)]
    acts = [sum(by_act[:f + 1]) for f in range(NT)]
    dves = [f + 1 - acts[f] for f in range(NT)]

    with nc.Block() as block:
        @block.sync
        def _(sp):
            sp.dma_start(k.mem[:, M_COL:M_COL + NCOL], dram["cols"]).then_inc(k.s_cols, 16)
            sp.dma_start(x_sb, dram["x"].rearrange("(t p) d -> p t d", p=P)).then_inc(s_x, 16)
            for n, (kind, b) in enumerate(ITEMS):
                if n >= NSLOT:
                    items_done(sp, k, n - NSLOT + 1)
                at = b * 512 if kind == "ada" else IN_AT[b]
                src = dram["w_ada" if kind == "ada" else "w_in"][:, at:at + 512]
                sp.dma_start(k.view((n % NSLOT) * SLOT, KC, 512),
                             src.rearrange("(c p) n -> p c n", p=P)).then_inc(s_slot[n % NSLOT], 16)
                if n == 3:
                    sp.dma_start(k.mem[:, M_C:M_C + NCONST], dram["consts"]).then_inc(k.s_const, 16)
                if n == 4:
                    sp.dma_start(w_ab, dram["w_in"][:, 4 * HW:4 * HW + 4 * NH].rearrange("(c p) n -> p c n", p=P)
                                 ).then_inc(s_ab_w, 16)
            n = len(ITEMS) - NSLOT
            assert n % NSLOT == A_BIAS // SLOT
            items_done(sp, k, n + 1)
            sp.dma_start(k.mem[:, A_BIAS:A_BIAS + NH * ROWS * QB], dram["bias"]).then_inc(k.s_bias, 16)

        @block.gpsimd
        def _(pool):
            for i in range(2):
                pool.memset(padded[i][:, 0:PAD], 0.0).then_inc(s_pad, 1)
                pool.memset(padded[i][:, PAD + T:PAD + T + PAD], 0.0).then_inc(s_pad, 1)

        @block.tensor
        def _(pe):
            tile = 0
            pe.wait_ge(s_cond, 1)
            for n, (kind, b) in enumerate(ITEMS):
                w = k.view((n % NSLOT) * SLOT, KC, 512)
                if kind == "in" and b == 0:
                    pe.wait_ge(k.s_const, 16)
                    for c in range(KC):
                        if c >= 6:
                            pe.wait_ge(s_hT, c - 5)
                        for t in range(TT):
                            if c == 0:
                                pe.wait_ge(s_xn, t + 1)
                            mm = pe.transpose(k.banks[2 + c % 6][:, t * P:(t + 1) * P],
                                              x_sb[:, t, c * P:(c + 1) * P], ident)
                        mm.then_inc(s_xT, 1)
                    pe.wait_ge(s_hT, KC)
                pe.wait_ge(s_slot[n % NSLOT], 16 * (n // NSLOT + 1))
                if kind == "ada":
                    bank = psA[b >= 4]
                    for m in range(4):
                        for c in range(KC):
                            mm = pe.matmul(bank[:, 4 * b + m:4 * b + m + 1], w[:, c, m * P:(m + 1) * P],
                                           cond[:, c:c + 1], start=(c == 0), stop=(c == KC - 1))
                    mm.then_inc(k.s_ada, 1)
                    continue
                for m in range(FC):
                    if tile >= RING:
                        f = tile - RING
                        if by_act[f]:
                            pe.wait_ge(s_evac, acts[f])
                        else:
                            pe.wait_ge(s_evacv, dves[f])
                    for c in range(KC):
                        mm = pe.matmul(psP[tile % RING][:, :], w[:, c, m * P:(m + 1) * P], hT[:, c, :],
                                       start=(c == 0), stop=(c == KC - 1))
                    mm.then_inc(k.s_tile, 1)
                    g = tile - NDN - 2 * FC
                    if g >= 0:
                        pe.wait_ge(s_sq, g + 1)
                        if g:
                            pe.wait_ge(s_inv, 2 * g - 1)
                        pe.matmul(psS[:, :], k.const("halves"), square[g % 2], start=True, stop=True).then_inc(s_ss, 1)
                    tile += 1
                if b == 0:
                    pe.wait_ge(s_ab_w, 16)
                    for s in range(STEPS):
                        for half, chunk in ((0, s), (1, STEPS - 1 - s)):
                            for c in range(KC):
                                mm = pe.matmul(psG[half * CH:(half + 1) * CH, s * 32:(s + 1) * 32],
                                               hT[:, c, chunk * CH:(chunk + 1) * CH], w_ab[:, c, :],
                                               start=(c == 0), stop=(c == KC - 1))
                    mm.then_inc(s_ab, 1)

        @block.scalar
        def _(act):
            act.wait_ge(k.s_cols, 16)
            act.activation(cond, k.col(C_C, KC), ACT.Silu).then_inc(s_cond, 1)
            act.wait_ge(s_x, 16)
            for t in range(TT):
                if t:
                    act.wait_ge(s_stat, t)
                act.activation(junk, x_sb[:, t, :], ACT.Square, accum_out=stat[:, t:t + 1]).then_inc(s_stat, 1)
            act.wait_ge(s_rstd, 2)
            act.activation(rstd, rstd, ACT.Sqrt).then_inc(s_rstd, 1)
            act.wait_ge(s_mod, 2)
            for c in range(KC):
                act.wait_ge(s_xT, c + 1)
                act.activation(hT[:, c, :], k.banks[2 + c % 6][:, :], ACT.Identity, bias=k.mod[:, c:c + 1],
                               scale=amod[:, c:c + 1]).then_inc(s_hT, 1)

            act.wait_ge(s_pad, 4)
            for f in range(NDN + 1):
                if f < NDN:
                    act.wait_ge(k.s_tile, f + 1)
                    if f >= 2:
                        act.wait_ge(s_tap, CONV * (f - 1))
                    act.activation(padded[f % 2][:, PAD:PAD + T], psP[f % RING][:, :], ACT.Copy).then_inc(s_evac, 1)
                if f >= 1:
                    act.wait_ge(s_tap, CONV * f)
                    act.activation(qkv[:, f - 1, :], conv[(f - 1) % 2], ACT.Silu).then_inc(s_silu, 1)
            for f in range(NDN, NDN + FC):
                act.wait_ge(k.s_tile, f + 1)
                act.activation(zT[:, f - NDN, :], psP[f % RING][:, :], ACT.Silu).then_inc(s_evac, 1)
            act.wait_ge(s_gate, 7)
            act.activation(gabs, gabs, ACT.Exp, scale=-1.0).then_inc(s_gact, 1)
            act.activation(gb, gb, ACT.Exp, scale=-1.0).then_inc(s_gact, 1)
            act.activation(expa, k.col(C_ALOG, NH), ACT.Exp).then_inc(s_gact, 1)
            act.wait_ge(s_gact, 3)
            act.activation(gabs, gabs, ACT.Ln, bias=1.0).then_inc(s_gact, 1)
            for f in range(NDN + FC, NDN + 2 * FC):
                act.wait_ge(k.s_tile, f + 1)
                act.activation(na[:, f - NDN - FC, :].rearrange("p (i r c) -> p r i c", r=ROWS, c=WIN),
                               psP[f % RING][:, :].rearrange("p (r i c) -> p r i c", r=ROWS, c=WIN),
                               ACT.Copy, scale=HD ** -0.5).then_inc(s_evac, 1)
                g = f - NDN - FC
                if g < 2:
                    act.wait_ge(s_silu, g + 1)
                    act.activation(square[g % 2], qkv[:, g, :], ACT.Square).then_inc(s_sq, 1)
            for g in range(2 * FC):
                act.wait_ge(s_inv, 2 * g + 2)
                if g:
                    act.wait_ge(k.s_norm, g)
                act.activation(inv, inv, ACT.Sqrt).then_inc(s_root, 1)
                if g + 2 < 2 * FC:
                    act.wait_ge(s_ss, g + 1)
                    act.activation(square[g % 2], qkv[:, g + 2, :], ACT.Square).then_inc(s_sq, 1)

        @block.vector
        def _(dve):
            dve.wait_ge(s_stat, TT)
            dve.tensor_scalar(rstd, stat, 1.0 / D, EPS, ALU.mult, ALU.add).then_inc(s_rstd, 1)
            dve.wait_ge(s_rstd, 1)
            dve.reciprocal(rstd, rstd).then_inc(s_rstd, 1)
            dve.wait_ge(s_rstd, 3)
            for t in range(TT):
                dve.tensor_scalar(x_sb[:, t, :], x_sb[:, t, :], rstd[:, t:t + 1], None, ALU.mult).then_inc(s_xn, 1)
            dve.wait_ge(k.s_ada, 4)
            dve.tensor_tensor(k.mod[:, 0:16], psA[0][:, 0:16], k.col(C_BADA, 16), ALU.add).then_inc(s_mod, 1)
            dve.wait_ge(s_mod, 1)
            dve.scalar_tensor_tensor(amod, k.mod[:, 8:16], 1.0, k.col(C_G1, KC), ALU.add, ALU.mult).then_inc(s_mod, 1)
            for f in range(NDN):
                dve.wait_ge(s_evac, f + 1)
                if f >= 2:
                    dve.wait_ge(s_silu, f - 1)
                src, dst = padded[f % 2], conv[f % 2]
                for t in range(CONV):
                    w = k.col(C_CONV + f * CONV + t)
                    if t == 0:
                        ins = dve.tensor_scalar(dst, src[:, 0:T], w, None, ALU.mult)
                    else:
                        dve.wait_ge(s_tap, CONV * f + t)
                        ins = dve.scalar_tensor_tensor(dst, src[:, t:t + T], w, dst, ALU.mult, ALU.add)
                    ins.then_inc(s_tap, 1)
                if f == 3:
                    dve.wait_ge(s_ab, 1)
                    ab = psG[:, 0:STEPS * 32].rearrange("p (s g) -> p s g", g=32)
                    for half in range(2):
                        rows = slice(half * CH, (half + 1) * CH)
                        dt = k.col(C_DT, NH)[rows].unsqueeze(1).to_broadcast([CH, STEPS, NH])
                        dve.tensor_tensor(ga[rows], ab[rows, :, half * NH:(half + 1) * NH], dt,
                                          ALU.add).then_inc(s_gate, 1)
                        dve.tensor_copy(gb[rows], ab[rows, :, (2 + half) * NH:(3 + half) * NH]).then_inc(s_gate, 1)
                    dve.wait_ge(s_gate, 4)
                    dve.tensor_scalar(gabs, ga, -1.0, None, ALU.mult).then_inc(s_gate, 1)
                    dve.wait_ge(s_gate, 5)
                    dve.tensor_tensor(gabs, gabs, ga, ALU.max).then_inc(s_gate, 1)
                    dve.wait_ge(s_gate, 6)
                    dve.tensor_scalar(ga, ga, 0.0, None, ALU.max).then_inc(s_gate, 1)
            dve.wait_ge(s_gact, 4)
            dve.tensor_tensor(ga, ga, gabs, ALU.add).then_inc(s_gate, 1)
            dve.tensor_scalar(gb, gb, 1.0, None, ALU.add).then_inc(s_gate, 1)
            dve.wait_ge(s_gate, 9)
            dve.scalar_tensor_tensor(k.g, ga, -1.0, expa.unsqueeze(1).to_broadcast([P, STEPS, NH]),
                                     ALU.mult, ALU.mult).then_inc(s_gate, 1)
            dve.reciprocal(k.beta, gb).then_inc(s_gate, 1)
            for f in range(NDN + 2 * FC, NT):
                dve.wait_ge(k.s_tile, f + 1)
                dve.tensor_copy(na[:, f - NDN - FC, :].rearrange("p (b r c) -> p r b c", r=ROWS, c=KB),
                                psP[f % RING][:, :].rearrange("p (r b c) -> p r b c", r=ROWS, c=KB)
                                ).then_inc(s_evacv, 1)
                g = f - NDN - 2 * FC
                dve.wait_ge(s_ss, g + 1)
                if g:
                    dve.wait_ge(k.s_norm, g)
                dve.tensor_scalar(inv, psS[:, :], EPS, None, ALU.add).then_inc(s_inv, 1)
                dve.wait_ge(s_inv, 2 * g + 1)
                dve.reciprocal(inv, inv).then_inc(s_inv, 1)
                dve.wait_ge(s_root, g + 1)
                dve.scalar_tensor_tensor(qkv[:, g, :], inv, HD ** -0.5 if g < FC else 1.0, qkv[:, g, :],
                                         ALU.mult, ALU.mult).then_inc(k.s_norm, 1)
            dve.wait_ge(k.s_ada, 12)
            dve.tensor_tensor(k.mod[:, 16:48], psA[1][:, 16:48], k.col(C_BADA + 16, 32), ALU.add).then_inc(s_mod, 1)


WINDOW = [(0, 0), (1, 1), (3, 1), (4, 2)]
PAIRS = sorted({w + 2 * m for w, _ in WINDOW for m in range(2)})
DELTA = [0, -WIN // 2, -WIN]
A_KZ = 0
A_BIAS = SLOT
A_V = 2 * SLOT
A_MASKED = 3 * SLOT
A_P = M_HT
A_PT = M_HT + 4 * 512


def attend(k):
    nc = k.nc
    naq, nak, nav = (k.view(M_NA + i * FC * T, FC, T) for i in range(3))
    mix = k.view(M_MIX, 2 * FC, T)
    kz = k.view(A_KZ, FC, 2, T)
    bias = k.view(A_BIAS, NH, ROWS, QB)
    vw = k.view(A_V, len(PAIRS), HW)
    masked = k.view(A_MASKED, 3, NH, ROWS * WC)
    prob = [k.view(A_P + i * 512, 2, ROWS * WC) for i in range(4)]
    probT = [k.view(A_PT + i * 512, 2, 2, P) for i in range(4)]
    ident, window = k.const("ident"), k.const("window")
    negmax, total, inverse = k.misc(4, 2), k.misc(4, 2), k.misc(4, 2)

    s_kz = k.sem("s_kz")
    s_masked = k.sem("s_masked")
    s_vt = k.sem("s_vt")
    s_vw = k.sem("s_vw")
    s_score = k.sem("s_score")
    s_biased = k.sem("s_biased")
    s_max = k.sem("s_max")
    s_exp = k.sem("s_exp")
    s_recip = k.sem("s_recip")
    s_prob = k.sem("s_prob")
    s_pt = k.sem("s_pt")
    s_ptout = k.sem("s_ptout")
    s_head = k.sem("s_head")
    s_headout = k.sem("s_headout")

    units = [(i, cc) for i in range(len(WINDOW)) for cc in range(FC)]
    N = len(units)
    psS = k.banks[0:3]
    psT = k.banks[3:5]
    psO = k.banks[5:7]

    with nc.Block() as block:
        @block.gpsimd
        def _(pool):
            for cc in range(FC):
                for hp in range(2):
                    own, other = slice(hp * HD, (hp + 1) * HD), slice((1 - hp) * HD, (2 - hp) * HD)
                    pool.tensor_copy(kz[own, cc, hp, :], nak[own, cc, :]).then_inc(s_kz, 1)
                    pool.memset(kz[other, cc, hp, :], 0.0).then_inc(s_kz, 1)
            pool.wait_ge(s_kz, 4 * FC)
            pool.wait_ge(k.s_bias, 16)
            for d, delta in enumerate(DELTA):
                at = WIN + delta
                for h in range(NH):
                    for b in range(WC // KB):
                        m = window[:, d * WC + b * KB:d * WC + (b + 1) * KB].unsqueeze(1).to_broadcast([P, ROWS, KB])
                        ins = pool.tensor_tensor(
                            masked[:, d, h, b * ROWS * KB:(b + 1) * ROWS * KB].rearrange("p (r c) -> p r c", c=KB),
                            bias[:, h, :, at + b * KB:at + (b + 1) * KB], m, ALU.add)
                        ins.then_inc(s_masked, 1)

        @block.tensor
        def _(pe):
            for j, b in enumerate(PAIRS):
                if j >= 2:
                    pe.wait_ge(s_vw, j - 1)
                for cc in range(FC):
                    mm = pe.transpose(psT[j % 2][:, cc * P:(cc + 1) * P],
                                      nav[:, cc, b * ROWS * KB:b * ROWS * KB + P], ident)
                mm.then_inc(s_vt, 1)
            for u in range(N + 3):
                if u < N:
                    i, cc = units[u]
                    if i == 0:
                        pe.wait_ge(s_kz, 4 * (cc + 1))
                    if u >= 3:
                        pe.wait_ge(s_biased, u - 2)
                    at = WINDOW[i][0] * ROWS * KB
                    pe.matmul(psS[u % 3][:, :], naq[:, cc, i * P:(i + 1) * P], kz[:, cc, :, at:at + ROWS * WC],
                              start=True, stop=True).then_inc(s_score, 1)
                v = u - 2
                if 0 <= v < N:
                    pe.wait_ge(s_prob, 2 * v + 2)
                    if v < 2:
                        pe.wait_ge(s_vw, len(PAIRS))
                    else:
                        pe.wait_ge(s_ptout, v - 1)
                    for hp in range(2):
                        for m in range(2):
                            mm = pe.transpose(psT[v % 2][:, (2 * hp + m) * P:(2 * hp + m + 1) * P],
                                              prob[v % 4][:, hp, m * P:(m + 1) * P], ident)
                    mm.then_inc(s_pt, 1)
                v = u - 3
                if v >= 0:
                    i, cc = units[v]
                    pe.wait_ge(s_ptout, v + 1)
                    if v >= 2:
                        pe.wait_ge(s_headout, v - 1)
                    for m in range(2):
                        for hp in range(2):
                            h = 2 * cc + hp
                            mm = pe.matmul(psO[v % 2][hp * HD:(hp + 1) * HD, 0:P],
                                           vw[:, PAIRS.index(WINDOW[i][0] + 2 * m), h * HD:(h + 1) * HD], probT[v % 4][:, hp, m, :],
                                           start=(m == 0), stop=(m == 1))
                    mm.then_inc(s_head, 1)

        @block.vector
        def _(dve):
            for u in range(N + 1):
                if u < N:
                    i, cc = units[u]
                    d = WINDOW[i][1]
                    dve.wait_ge(s_score, u + 1)
                    dve.wait_ge(s_masked, (d * NH + 2 * cc + 2) * (WC // KB))
                    if u >= 4:
                        dve.wait_ge(s_pt, u - 3)
                    dve.tensor_tensor(prob[u % 4].rearrange("p h k -> p (h k)"), psS[u % 3][:, :],
                                      masked[:, d, 2 * cc:2 * cc + 2, :].rearrange("p h k -> p (h k)"),
                                      ALU.add).then_inc(s_biased, 1)
                    dve.wait_ge(s_biased, u + 1)
                    dve.tensor_reduce(negmax[:, u % 4, :], prob[u % 4], AX.X, ALU.max, negate=True).then_inc(s_max, 1)
                if u >= 1:
                    v = u - 1
                    dve.wait_ge(s_exp, 2 * v + 2)
                    dve.reciprocal(inverse[:, v % 4, :], total[:, v % 4, :]).then_inc(s_recip, 1)
                    dve.wait_ge(s_recip, v + 1)
                    for hp in range(2):
                        dve.tensor_scalar(prob[v % 4][:, hp, :], prob[v % 4][:, hp, :], inverse[:, v % 4, hp:hp + 1],
                                          None, ALU.mult).then_inc(s_prob, 1)

        @block.scalar
        def _(act):
            for j in range(len(PAIRS)):
                act.wait_ge(s_vt, j + 1)
                act.activation(vw[:, j, :], psT[j % 2][:, :], ACT.Copy).then_inc(s_vw, 1)
            for u in range(N + 3):
                if u < N:
                    act.wait_ge(s_max, u + 1)
                    for hp in range(2):
                        act.activation(prob[u % 4][:, hp, :], prob[u % 4][:, hp, :], ACT.Exp,
                                       bias=negmax[:, u % 4, hp:hp + 1],
                                       accum_out=total[:, u % 4, hp:hp + 1]).then_inc(s_exp, 1)
                v = u - 2
                if 0 <= v < N:
                    act.wait_ge(s_pt, v + 1)
                    if v >= 4:
                        act.wait_ge(s_head, v - 3)
                    act.activation(probT[v % 4].rearrange("p h m q -> p (h m q)"), psT[v % 2][:, :],
                                   ACT.Copy).then_inc(s_ptout, 1)
                v = u - 3
                if v >= 0:
                    i, cc = units[v]
                    act.wait_ge(s_head, v + 1)
                    act.activation(mix[:, FC + cc, :].rearrange("p (r c) -> p r c", c=GRID_W)[
                                       :, :, i * WIN:(i + 1) * WIN],
                                   psO[v % 2][:, 0:P].rearrange("p (r c) -> p r c", c=WIN),
                                   ACT.Copy).then_inc(s_headout, 1)


BLK = NH * P
D_TOKENS = 0
D_HEADS = D_TOKENS + 3 * FC * P
D_MA = D_HEADS + FC * 2 * 2 * P
D_U, D_T, D_X, D_KG, D_KT, D_QT = (D_MA + (2 + i) * BLK for i in range(6))
D_V, D_NEW, D_NEWT = (D_QT + BLK + i * HW for i in range(3))
D_SET = D_QT + BLK + 3 * HW
D_STATE = 2 * D_SET
D_DECAY = D_STATE + 2 * HW
D_MASKED = M_NA + 2 * FC * T
HALVES = (slice(0, CH), slice(CH, P))
JOINS = LEVELS - 1
START = 1
INV = 3 * JOINS


def delta(k):
    nc = k.nc
    qkv = k.view(M_QKV, 3 * FC, T)
    mix = k.view(M_MIX, 2 * FC, T)
    zT = k.view(M_Z, FC, T)
    ident, uptoc, fold, levels = (k.const(n) for n in ("ident", "uptoc", "fold", "levels"))
    egc, etail, elast = k.misc(STEPS * NH), k.misc(STEPS * NH), k.misc(STEPS * NH)
    g_flat = k.g.rearrange("p s h -> p (s h)")
    beta_flat = k.beta.rearrange("p s h -> p (s h)")
    squares = k.view(M_NA, FC, T)
    inv = k.view(M_NA + FC * T, FC, T)

    class Stream:
        def __init__(self, s):
            def buf(at, *shape):
                return k.view(s * D_SET + at, *shape)
            self.tokens = buf(D_TOKENS, 3 * FC, 2, CH)
            self.heads = buf(D_HEADS, FC, 2, 2, P)
            self.ma = buf(D_MA, NH, 2, P)
            self.u, self.t, self.x, self.kg, self.kt, self.qt = (
                buf(at, NH, P) for at in (D_U, D_T, D_X, D_KG, D_KT, D_QT))
            self.w, self.qg = self.t, self.x
            self.v, self.new = buf(D_V, NH, HD), buf(D_NEW, NH, HD)
            self.newT = buf(D_NEWT, FC, P)
            self.g = k.view(D_MASKED + 2 * s * HW, NH, CH)
            self.beta = k.view(D_MASKED + (2 * s + 1) * HW, NH, CH)
            self.e = k.view(D_DECAY + s * HW, NH, CH)
            self.banks = k.banks[4 * s:4 * s + 4]
            self.old = k.view(D_STATE + s * HW, NH, HD)
            self.next = k.view(D_STATE + (1 - s) * HW, NH, HD)
            names = ("staged", "decay", "score", "exp", "em", "ma", "tok", "v", "kg", "qg", "u0", "w", "wout",
                     "q", "qout", "new", "newTout", "newp", "newout", "o", "oout", "ds", "dsout", "dst",
                     "scaled", "state")
            self.s = {n: k.sem(f"s_{n}{s}") for n in names}
            self.inv = [k.sem(f"s_inv{s}{h}") for h in range(2)]
            self.copied = [k.sem(f"s_copied{s}{h}") for h in range(2)]
            self.joined = [k.sem(f"s_joined{s}{h}") for h in range(2)]

    streams = [Stream(0), Stream(1)]
    other = {0: streams[1], 1: streams[0]}
    s_zero = k.sem("s_zero")
    s_sums = k.sem("s_sums")
    s_esums = k.sem("s_esums")
    s_tailb = k.sem("s_tailb")
    s_turn = k.sem("s_turn")
    s_turnp = k.sem("s_turnp")
    s_oready = k.sem("s_oready")
    s_osq = k.sem("s_osq")
    s_oss = k.sem("s_oss")
    s_oinv = k.sem("s_oinv")
    s_oroot = k.sem("s_oroot")
    s_omul = k.sem("s_omul")
    ITS = STEPS // 2
    ZEROED = 2 * 8 + 1 + 1

    def flat(ap):
        return ap.rearrange("p a b -> p (a b)")

    def heads4(bank):
        return bank[:, :].rearrange("p (h j) -> p h j", j=P)

    with nc.Block() as block:
        @block.gpsimd
        def _(pool):
            for st in streams:
                for b in (st.heads.rearrange("p a b c d -> p (a b c d)"), st.ma.rearrange("p a b c -> p (a b c)"),
                          flat(st.u), flat(st.t), flat(st.x), flat(st.kg), flat(st.kt), flat(st.qt)):
                    pool.memset(b, 0.0).then_inc(s_zero, 1)
            pool.memset(flat(streams[0].old), 0.0).then_inc(s_zero, 1)
            pool.memset(flat(mix[:, 0:FC, :]), 0.0).then_inc(s_zero, 1)
            pool.wait_ge(s_zero, ZEROED)
            with pool.Fori(0, ITS) as it:
                for s, st in enumerate(streams):
                    step = it * 2 + s
                    pool.wait_ge(st.s["decay"], it + START)
                    pool.wait_ge(st.s["score"], it * FC + START)
                    pool.wait_ge(st.s["tok"], it * 3 + START)
                    g = g_flat[:, bass.ds(step * NH, NH)].unsqueeze(2).to_broadcast([P, NH, CH])
                    b = beta_flat[:, bass.ds(step * NH, NH)].unsqueeze(2).to_broadcast([P, NH, CH])
                    cols = uptoc.unsqueeze(1).to_broadcast([P, NH, CH])
                    pool.tensor_tensor(st.g, g, cols, ALU.mult).then_inc(st.s["staged"], 1)
                    starts = (step * CH, (STEPS - 1) * CH - step * CH)
                    for d, start in enumerate(starts):
                        pool.tensor_copy(st.tokens[:, :, d, :], qkv[:, :, bass.ds(start, CH)]).then_inc(st.s["staged"], 1)
                    pool.wait_ge(st.s["staged"], it * 8 + 3)
                    pool.sem_inc(s_turnp, 1)
                    for hp in range(2):
                        own = HALVES[hp]
                        if hp:
                            pool.wait_ge(st.s["staged"], it * 8 + 5)
                            pool.sem_inc(s_turnp, 1)
                        for qk in range(2):
                            pool.tensor_copy(
                                st.heads[own, :, hp, qk, :],
                                st.tokens[own, qk * FC:(qk + 1) * FC].rearrange("p a b c -> p a (b c)")
                                ).then_inc(st.s["staged"], 1)
                    pool.wait_ge(st.s["staged"], it * 8 + 7)
                    pool.wait_ge(st.s["em"], it + START)
                    pool.tensor_tensor(st.beta, b, cols, ALU.mult).then_inc(st.s["staged"], 1)

        @block.tensor
        def _(pe):
            for st in streams:
                for name in ("decay", "score", "tok", "new", "o"):
                    pe.sem_inc(st.s[name], START)
            for i, name in enumerate(("upto", "after", "halves")):
                pe.matmul(k.banks[i][:, 0:STEPS * NH], k.const(name), g_flat, start=True, stop=True).then_inc(s_sums, 1)
            pe.wait_ge(s_esums, 3)
            pe.wait_ge(s_zero, ZEROED)
            with pe.Fori(0, ITS) as it:
                for st in streams:
                    s, b = st.s, st.banks
                    pe.wait_ge(s["staged"], it * 8 + 1)
                    pe.wait_ge(s["oout"], it * 2 + START)
                    pe.matmul(b[0][:, :], k.const("after"), flat(st.g), start=True, stop=True).then_inc(s["decay"], 1)
                    pe.wait_ge(s["staged"], it * 8 + 7)
                    for cc in range(FC):
                        if cc == 0:
                            pe.wait_ge(s["dsout"], it + START)
                        elif cc == 1:
                            pe.wait_ge(s["state"], it + START)
                        elif cc == 2:
                            pe.wait_ge(s["newout"], it + START)
                        else:
                            pe.wait_ge(s["exp"], it + 1)
                        pe.matmul(b[(cc + 1) % 4][:, :], st.tokens[:, FC + cc].rearrange("p a b -> p (a b)"),
                                  st.heads[:, cc].rearrange("p a b c -> p (a b c)"),
                                  start=True, stop=True).then_inc(s["score"], 1)
                    for i, part in enumerate((1, 2, 0)):
                        pe.wait_ge(s["ma"], it * 8 + 2 * (i + 1) + START)
                        for cc in range(FC):
                            mm = pe.transpose(b[i + 1][:, cc * P:(cc + 1) * P],
                                              st.tokens[:, part * FC + cc].rearrange("p a b -> p (a b)"), ident)
                        mm.then_inc(s["tok"], 1)
                for j in range(-1, JOINS):
                    for stage in ("X", "U", "T"):
                        if (j < 0 and stage != "T") or (j == JOINS - 1 and stage == "T"):
                            continue
                        for st in streams:
                            for half in range(2):
                                bank = heads4(st.banks[half])
                                if stage == "T":
                                    pe.wait_ge(st.joined[half], it * LEVELS + j + 2)
                                    if j < 0 and half == 0:
                                        pe.wait_ge(st.s["ma"], it * 8 + 8 + START)
                                    if j < 0 and half == 1:
                                        pe.wait_ge(st.s["kg"], it * 4 + 4)
                                elif stage == "X":
                                    pe.wait_ge(st.copied[half], it * (2 * JOINS) + 2 * j + 1)
                                else:
                                    pe.wait_ge(st.copied[half], it * (2 * JOINS) + 2 * j + 2)
                                for i in range(NH // 2):
                                    h = half * (NH // 2) + i
                                    if stage == "T":
                                        mm = pe.transpose(bank[:, i, :], st.u[:, h, :], ident)
                                    elif stage == "X":
                                        mm = pe.matmul(bank[:, i, :], st.ma[:, h, 1, :], st.t[:, h, :],
                                                       start=True, stop=True)
                                    else:
                                        mm = pe.matmul(bank[:, i, :], st.x[:, h, :], st.u[:, h, :],
                                                       start=True, stop=True)
                                mm.then_inc(st.inv[half], 1)
                for n, st in enumerate(streams):
                    s, b = st.s, st.banks
                    for half in range(2):
                        pe.wait_ge(st.joined[half], it * LEVELS + LEVELS)
                        pe.wait_ge(s["v"] if half == 0 else s["qg"], it + 1 if half == 0 else it * 2 + 2)
                        for i in range(NH // 2):
                            h = half * (NH // 2) + i
                            mm = pe.matmul(heads4(b[2 + half])[:, i, :], st.kg[:, h, :], st.u[:, h, :],
                                           start=True, stop=True)
                        mm.then_inc(s["w"], 1)
                    for half in range(2):
                        for i in range(NH // 2):
                            h = half * (NH // 2) + i
                            mm = pe.transpose(heads4(b[half])[:, i, :], st.qg[:, h, :], ident)
                        mm.then_inc(s["q"], 1)
                    pe.wait_ge(s["wout"], it * 2 + 2)
                    pe.wait_ge(other[n].s["state"], it + n + START)
                    for cc in range(FC):
                        for i in range(2):
                            for hp in range(2):
                                h = 2 * cc + hp
                                left, right = ((st.v, st.u), (st.old, st.w))[i]
                                mm = pe.matmul(b[2][hp * HD:(hp + 1) * HD, cc * P:(cc + 1) * P], left[:, h, :],
                                               right[:, h, :], start=(i == 0), stop=(i == 1))
                    mm.then_inc(s["new"], 1)
                    pe.wait_ge(s["newTout"], it + 1)
                    for cc in range(FC):
                        mm = pe.transpose(b[3][:, cc * P:(cc + 1) * P], st.newT[:, cc, :], ident)
                    mm.then_inc(s["newp"], 1)
                    pe.wait_ge(s["newout"], it + 1 + START)
                    pe.wait_ge(s["qout"], it * 2 + 2)
                    for cc in range(FC):
                        for hp in range(2):
                            h = 2 * cc + hp
                            mm = pe.matmul(b[1][hp * HD:(hp + 1) * HD, cc * P:(cc + 1) * P], st.new[:, h, :],
                                           st.kt[:, h, :], start=True, stop=True)
                    mm.then_inc(s["ds"], 1)
                    for cc in range(FC):
                        for i in range(2):
                            for hp in range(2):
                                h = 2 * cc + hp
                                left, right = ((st.old, st.qt[:, h, :]), (st.new, st.ma[:, h, 0, :]))[i]
                                mm = pe.matmul(b[0][hp * HD:(hp + 1) * HD, cc * P:(cc + 1) * P], left[:, h, :],
                                               right, start=(i == 0), stop=(i == 1))
                    mm.then_inc(s["o"], 1)
                    pe.wait_ge(s["dsout"], it + 1 + START)
                    for cc in range(FC):
                        mm = pe.transpose(b[2][:, cc * P:(cc + 1) * P], st.newT[:, cc, :], ident)
                    mm.then_inc(s["dst"], 1)
            pe.wait_ge(streams[1].s["state"], ITS + START)
            for cc in range(FC):
                pe.wait_ge(s_osq, cc + 1)
                pe.matmul(k.banks[4 + cc][:, :], k.const("halves"), squares[:, cc, :],
                          start=True, stop=True).then_inc(s_oss, 1)

        @block.scalar
        def _(act):
            for st in streams:
                for name in ("dsout", "newout"):
                    act.sem_inc(st.s[name], START)
            act.wait_ge(s_sums, 3)
            for i, e in enumerate((egc, etail, elast)):
                act.activation(e, k.banks[i][:, 0:STEPS * NH], ACT.Exp).then_inc(s_esums, 1)
            act.wait_ge(s_esums, 3)
            act.wait_ge(s_zero, ZEROED)
            with act.Fori(0, ITS) as it:
                for st in streams:
                    s, b = st.s, st.banks
                    act.wait_ge(s["decay"], it + 1 + START)
                    act.wait_ge(s["ma"], it * 8 + START)
                    act.activation(flat(st.e), b[0][:, :], ACT.Exp).then_inc(s["exp"], 1)
                for st in streams:
                    s, b = st.s, st.banks
                    act.wait_ge(s["tok"], it * 3 + 2 + START)
                    act.wait_ge(s["new"], it + START)
                    act.activation(flat(st.v), b[2][:, :], ACT.Copy).then_inc(s["v"], 1)
                for j in range(-1, JOINS):
                    for stage in ("X", "T"):
                        if (j < 0 and stage == "X") or (j == JOINS - 1 and stage == "T"):
                            continue
                        for st in streams:
                            for half in range(2):
                                hs = slice(half * NH // 2, (half + 1) * NH // 2)
                                count = (3 * JOINS) * it + 3 * j + (2 if stage == "X" else 4)
                                act.wait_ge(st.inv[half], count)
                                if stage == "X":
                                    act.activation(flat(st.x[:, hs]), st.banks[half][:, :], ACT.Copy,
                                                   scale=-1.0).then_inc(st.copied[half], 1)
                                else:
                                    act.activation(flat(st.t[:, hs]), st.banks[half][:, :],
                                                   ACT.Copy).then_inc(st.copied[half], 1)
                for st in streams:
                    s, b = st.s, st.banks
                    for half in range(2):
                        hs = slice(half * NH // 2, (half + 1) * NH // 2)
                        act.wait_ge(s["w"], it * 2 + half + 1)
                        act.activation(flat(st.w[:, hs]), b[2 + half][:, :], ACT.Copy, scale=-1.0).then_inc(s["wout"], 1)
                    for half in range(2):
                        hs = slice(half * NH // 2, (half + 1) * NH // 2)
                        act.wait_ge(s["q"], it * 2 + half + 1)
                        act.activation(flat(st.qt[:, hs]), b[half][:, :], ACT.Copy).then_inc(s["qout"], 1)
                    act.wait_ge(s["new"], it + 1 + START)
                    act.activation(flat(st.newT), b[2][:, :], ACT.Copy).then_inc(s["newTout"], 1)
                    act.wait_ge(s["newp"], it + 1)
                    act.activation(flat(st.new), b[3][:, :], ACT.Copy).then_inc(s["newout"], 1)
                    act.wait_ge(s["ds"], it + 1)
                    act.activation(flat(st.newT), b[1][:, :], ACT.Copy).then_inc(s["dsout"], 1)
            for st in streams:
                act.wait_ge(st.s["oout"], 2 * ITS + START)
            for cc in range(FC):
                act.activation(squares[:, cc, :], mix[:, cc, :], ACT.Square).then_inc(s_osq, 1)
            for cc in range(FC):
                act.wait_ge(s_oinv, 2 * cc + 2)
                act.activation(inv[:, cc, :], inv[:, cc, :], ACT.Sqrt).then_inc(s_oroot, 1)

        @block.vector
        def _(dve):
            for st in streams:
                for name in ("em", "oout", "state", "ma"):
                    dve.sem_inc(st.s[name], START)
            dve.wait_ge(s_esums, 3)
            dve.tensor_tensor(etail, etail, beta_flat, ALU.mult).then_inc(s_tailb, 1)
            dve.wait_ge(s_tailb, 1)
            dve.wait_ge(s_zero, ZEROED)
            with dve.Fori(0, ITS) as it:
                for n, st in enumerate(streams):
                    s, b = st.s, st.banks
                    step8 = it * (2 * NH) + n * NH
                    dve.wait_ge(s["exp"], it + 1)
                    dve.wait_ge(s["staged"], it * 8 + 8)
                    dve.tensor_tensor(st.e, st.e, st.beta, ALU.mult).then_inc(s["em"], 1)
                    dve.wait_ge(s["em"], it + 1 + START)
                    for cc in range(FC):
                        dve.wait_ge(s["score"], it * FC + cc + 1 + START)
                        scores = b[(cc + 1) % 4][:, :].rearrange("p (h m j) -> p h m j", h=2, m=2)
                        for d, rows in enumerate(HALVES):
                            c = slice(d * CH, (d + 1) * CH)
                            e = st.e[rows, 2 * cc:2 * cc + 2].unsqueeze(2).to_broadcast([CH, 2, 2, CH])
                            dve.tensor_tensor(st.ma[rows, 2 * cc:2 * cc + 2, :, c], scores[rows, :, :, c], e,
                                              ALU.mult).then_inc(s["ma"], 1)
                    dve.wait_ge(s["ma"], it * 8 + 8 + START)
                    for half in range(2):
                        hs = slice(half * NH // 2, (half + 1) * NH // 2)
                        for d, rows in enumerate(HALVES):
                            c = slice(d * CH, (d + 1) * CH)
                            mask = levels[rows, 0:CH].unsqueeze(1).to_broadcast([CH, NH // 2, CH])
                            dve.scalar_tensor_tensor(st.u[rows, hs, c], st.ma[rows, hs, 1, c], -1.0, mask,
                                                     ALU.mult, ALU.mult).then_inc(s["u0"], 1)
                        dve.wait_ge(s["u0"], it * 4 + 2 * half + 2)
                        dve.tensor_tensor(st.u[:, hs], st.u[:, hs], ident.unsqueeze(1).to_broadcast([P, NH // 2, P]),
                                          ALU.add).then_inc(st.joined[half], 1)
                    dve.wait_ge(s["tok"], it * 3 + 1 + START)
                    tok = b[1][:, :].rearrange("p (h j) -> p h j", j=HD)
                    for d, rows in enumerate(HALVES):
                        c = slice(d * CH, (d + 1) * CH)
                        for dst, e in ((st.kg, egc), (st.kt, etail)):
                            e = e[rows, bass.ds(step8, NH)].unsqueeze(2).to_broadcast([CH, NH, HD])
                            dve.tensor_tensor(dst[rows, :, c], tok[rows], e, ALU.mult).then_inc(s["kg"], 1)
                for j in range(JOINS):
                    for st in streams:
                        for half in range(2):
                            hs = slice(half * NH // 2, (half + 1) * NH // 2)
                            bank = heads4(st.banks[half])
                            dve.wait_ge(st.inv[half], it * INV + 3 * j + 3)
                            dve.wait_ge(st.joined[half], it * LEVELS + j + 1)
                            dve.sem_inc(s_turn, 1)
                            for d, rows in enumerate(HALVES):
                                c = slice(d * CH, (d + 1) * CH)
                                mask = levels[rows, (j + 1) * CH:(j + 2) * CH].bitcast(U32)
                                ins = dve.copy_predicated(st.u[rows, hs, c],
                                                          mask.unsqueeze(1).to_broadcast([CH, NH // 2, CH]),
                                                          bank[rows, :, c])
                            ins.then_inc(st.joined[half], 1)
                for n, st in enumerate(streams):
                    s, b = st.s, st.banks
                    step8 = it * (2 * NH) + n * NH
                    dve.wait_ge(s["tok"], it * 3 + 3 + START)
                    tok = b[3][:, :].rearrange("p (h j) -> p h j", j=HD)
                    for d, rows in enumerate(HALVES):
                        c = slice(d * CH, (d + 1) * CH)
                        e = egc[rows, bass.ds(step8, NH)].unsqueeze(2).to_broadcast([CH, NH, HD])
                        dve.tensor_tensor(st.qg[rows, :, c], tok[rows], e, ALU.mult).then_inc(s["qg"], 1)
                for n, st in enumerate(streams):
                    s, b = st.s, st.banks
                    step = it * 2 + n
                    step8 = it * (2 * NH) + n * NH
                    dve.wait_ge(other[n].s["state"], it + n + START)
                    dve.wait_ge(other[n].s["o"], it + n + START)
                    e = elast[:, bass.ds(step8, NH)].unsqueeze(2).to_broadcast([P, NH, HD])
                    dve.tensor_tensor(st.next, st.old, e, ALU.mult).then_inc(s["scaled"], 1)
                    dve.wait_ge(s["o"], it + 1 + START)
                    dve.wait_ge(other[n].s["oout"], 2 * it + 2 * n + START)
                    o = b[0][:, :].rearrange("p (a d c) -> p a d c", d=2, c=CH)
                    for d, start in enumerate((step * CH, (STEPS - 1) * CH - step * CH)):
                        at = mix[:, 0:FC, bass.ds(start, CH)]
                        dve.tensor_tensor(at, at, o[:, :, d, :], ALU.add).then_inc(s["oout"], 1)
                    dve.wait_ge(s["dst"], it + 1)
                    dve.wait_ge(s["scaled"], it + 1)
                    dve.tensor_tensor(flat(st.next), flat(st.next), b[2][:, :], ALU.add).then_inc(s["state"], 1)
            for cc in range(FC):
                dve.wait_ge(s_oss, cc + 1)
                dve.tensor_scalar(inv[:, cc, :], k.banks[4 + cc][:, :], 1.0 / HD, EPS, ALU.mult, ALU.add).then_inc(s_oinv, 1)
                dve.wait_ge(s_oinv, 2 * cc + 1)
                dve.reciprocal(inv[:, cc, :], inv[:, cc, :]).then_inc(s_oinv, 1)
            for cc in range(FC):
                dve.scalar_tensor_tensor(mix[:, cc, :], mix[:, cc, :], k.col(C_ONORM), zT[:, cc, :],
                                         ALU.mult, ALU.mult).then_inc(s_omul, 1)
                dve.wait_ge(s_oroot, cc + 1)
                dve.wait_ge(s_omul, 2 * cc + 1)
                dve.tensor_tensor(mix[:, cc, :], mix[:, cc, :], inv[:, cc, :], ALU.mult).then_inc(s_omul, 1)


def load_expert(sp, k, e, parity, static=True):
    for i, (name, rows) in enumerate((("w_gate", KC), ("w_up", KC), ("w_down", DE // P))):
        src = k.dram[name][e] if static else k.dram[name][bass.ds(e, 1)].rearrange("a r n -> (a r) n")
        sp.dma_start(k.view((3 * parity + i) * SLOT, rows, SLOT // rows),
                     src.rearrange("(c p) n -> p c n", p=P)).then_inc(k.s_expert[parity][i], 16)


M_X1 = M_NA
M_GT1 = M_NA + TT * D
M_GT2 = M_GT1 + D
M_A2 = M_Z
M_B2 = M_Z + D
M_H2 = M_QKV
M_DIAG = M_QKV + TT * D
W_OUT_AT = 4 * SLOT
ITEMS_MAX = NE + 2 * T // SL
ROWS_OUT = 2 * T


def route(k):
    nc, dram = k.nc, k.dram
    mixT = k.view(M_MIX, KC, T)
    w_out = [k.view(W_OUT_AT + i * SLOT, KC, 512) for i in range(2)]
    w_route = k.view(M_WAB, KC, NG + NE)
    x1 = k.view(M_X1, TT, D)
    h2 = k.view(M_H2, TT, D)
    h2T = k.view(M_HT, KC, T)
    rows = k.view(M_GT1, D), k.view(M_A2, D), k.view(M_B2, D), k.view(M_GT2, D)
    diag = [k.view(M_DIAG + i * P, P) for i in range(4)]
    junk = k.view(M_DIAG + 512, D)
    logitsT = k.view(M_DIAG + 1536, T)
    ident = k.const("ident")
    k.misc_at = k.free_misc
    k.weight = [k.misc(TT), k.misc(TT)]
    k.row = [k.misc(TT).bitcast(I32), k.misc(TT).bitcast(I32)]
    k.place = k.misc(TT, NE)
    k.item_e, k.item_place, k.item_row = (k.misc(ITEMS_MAX + 1).bitcast(I32) for _ in range(3))
    k.tiles = k.misc(NE).bitcast(I32)
    k.upto = k.misc(NE).bitcast(I32)
    k.total = k.upto[:, NE - 1:NE]
    col = k.misc(3 * KC)
    ss, ss2, rs = k.misc(2, TT), k.misc(TT), k.misc(2, TT)
    logits = k.misc(TT, NG + NE)
    first = k.misc(EG)
    gmax, gexp, gsum, geq, gbest, gone = k.misc(TT), k.misc(TT, NG), k.misc(TT), k.misc(TT, NG), k.misc(TT), k.misc(TT, NG)
    per_group, ing = k.misc(TT, NG, EG), k.misc(TT, EG)
    top, eq, best = [k.misc(TT), k.misc(TT)], k.misc(TT, EG), k.misc(TT)
    one = [k.misc(TT, EG), k.misc(TT, EG)]
    chosen = [k.misc(TT, NE), k.misc(TT, NE)]
    ratio, denom = k.misc(TT), k.misc(TT)
    both, both_sum = k.misc(TT, NE), k.misc(NE)
    rank, base = k.view(M_DIAG + 512, TT, NE), k.view(M_DIAG + 512 + TT * NE, TT, NE)
    rowf = [k.misc(TT), k.misc(TT)]
    count, over, tiles = k.misc(NE), k.view(M_DIAG, NE, T // SL - 1), k.misc(NE)
    cum, before = [k.misc(2, NE), k.misc(2, NE)], k.misc(NE)
    expert, place, row = (k.misc(ITEMS_MAX + 1) for _ in range(3))
    past = k.view(M_HT, ITEMS_MAX + 1, NE)
    spare = k.view(M_HT + 2048, ITEMS_MAX + 1, NE)

    s_wo = [k.sem("s_wo0"), k.sem("s_wo1")]
    s_x1in = k.sem("s_x1in")
    s_wr = k.sem("s_wr")
    s_col = k.sem("s_col")
    s_diag = k.sem("s_diag")
    s_row = k.sem("s_row")
    s_rowout = k.sem("s_rowout")
    s_y = k.sem("s_y")
    s_ysq = k.sem("s_ysq")
    s_yms = k.sem("s_yms")
    s_yroot = k.sem("s_yroot")
    s_yout = k.sem("s_yout")
    s_x1 = k.sem("s_x1")
    s_xsq = k.sem("s_xsq")
    s_h2 = k.sem("s_h2")
    s_h2T = k.sem("s_h2T")
    s_h2Tout = k.sem("s_h2Tout")
    s_logit = k.sem("s_logit")
    s_logitout = k.sem("s_logitout")
    s_logitp = k.sem("s_logitp")
    s_r = k.sem("s_r")
    s_rexp = k.sem("s_rexp")
    s_both = k.sem("s_both")
    s_rank = k.sem("s_rank")
    s_xms = k.sem("s_xms")
    s_xroot = k.sem("s_xroot")
    s_gshift = k.sem("s_gshift")
    s_diff = k.sem("s_diff")

    psY = [k.banks[0:2], k.banks[2:4]]
    psT = k.banks[4:6]
    psR = k.banks[6]
    psL = k.banks[7]

    with nc.Block() as block:
        @block.sync
        def _(sp):
            for i in range(2):
                sp.dma_start(w_out[i], dram["w_out"][:, i * 512:(i + 1) * 512].rearrange("(c p) n -> p c n", p=P)
                             ).then_inc(s_wo[i], 16)
            sp.dma_start(x1, dram["x"].rearrange("(t p) d -> p t d", p=P)).then_inc(s_x1in, 16)
            sp.dma_start(w_route, dram["w_route"].rearrange("(c p) n -> p c n", p=P)).then_inc(s_wr, 16)
            load_expert(sp, k, 0, 0)

        @block.tensor
        def _(pe):
            for n in range(4 * KC):
                pe.wait_ge(s_diag, n + 1)
                if n % 4 == 0 and n >= 4:
                    pe.wait_ge(s_rowout, n // 4)
                pe.matmul(psR[:, (n % 4) * P:(n % 4 + 1) * P], k.const("ones"), diag[n % 4],
                          start=True, stop=True).then_inc(s_row, 1)
            for t in range(TT + 1):
                if t < TT:
                    for i in range(2):
                        if t == 0:
                            pe.wait_ge(s_wo[i], 16)
                        if t >= 2:
                            pe.wait_ge(s_yout, 2 * (t - 2) + i + 1)
                        for c in range(KC):
                            mm = pe.matmul(psY[t % 2][i][:, :], mixT[:, c, t * P:(t + 1) * P], w_out[i][:, c, :],
                                           start=(c == 0), stop=(c == KC - 1))
                        mm.then_inc(s_y, 1)
                if t >= 1:
                    pe.wait_ge(s_h2, 2 * t)
                    for c in range(KC):
                        if c % 4 == 0 and t > 1:
                            pe.wait_ge(s_h2Tout, 2 * (t - 2) + c // 4 + 1)
                        mm = pe.transpose(psT[c // 4][:, (c % 4) * P:(c % 4 + 1) * P],
                                          h2[:, t - 1, c * P:(c + 1) * P], ident)
                        if c % 4 == 3:
                            mm.then_inc(s_h2T, 1)
            pe.wait_ge(s_wr, 16)
            pe.wait_ge(s_h2Tout, 2 * TT)
            for c in range(KC):
                mm = pe.matmul(psL[0:NG + NE, :], w_route[:, c, :], h2T[:, c, :], start=(c == 0), stop=(c == KC - 1))
            mm.then_inc(s_logit, 1)
            pe.wait_ge(s_logitout, 1)
            pe.wait_ge(s_rowout, KC)
            for t in range(TT):
                mm = pe.transpose(psR[:, t * 64:t * 64 + NG + NE], logitsT[0:NG + NE, t * P:(t + 1) * P],
                                  ident[0:NG + NE, 0:NG + NE])
            mm.then_inc(s_logitp, 1)
            pe.wait_ge(s_both, 1)
            pe.matmul(psT[0][:, 0:NE], k.const("before"), both_sum, start=True, stop=True).then_inc(s_rank, 1)
            pe.matmul(psT[1][:, 0:NE], k.const("ones"), both_sum, start=True, stop=True).then_inc(s_rank, 1)

        @block.scalar
        def _(act):
            for t in range(TT + 1):
                if t < TT:
                    for i in range(2):
                        act.wait_ge(s_y, 2 * t + i + 1)
                        if t or i:
                            act.wait_ge(s_ysq, 2 * t + i)
                        if t and i == 0:
                            act.wait_ge(s_xsq, t)
                        act.activation(junk[:, 0:512], psY[t % 2][i][:, :], ACT.Square,
                                       accum_out=ss[:, i, t:t + 1]).then_inc(s_ysq, 1)
                    act.wait_ge(s_yms, 3 * (t + 1))
                    act.activation(rs[:, 0, t:t + 1], rs[:, 0, t:t + 1], ACT.Sqrt).then_inc(s_yroot, 1)
                    act.wait_ge(s_x1, t + 1)
                    act.wait_ge(s_ysq, 2 * t + 2)
                    act.activation(junk, x1[:, t, :], ACT.Square, accum_out=ss2[:, t:t + 1]).then_inc(s_xsq, 1)
                    act.wait_ge(s_xms, 2 * (t + 1))
                    act.activation(rs[:, 1, t:t + 1], rs[:, 1, t:t + 1], ACT.Sqrt).then_inc(s_xroot, 1)
                if t >= 1:
                    for i in range(2):
                        act.wait_ge(s_h2T, 2 * (t - 1) + i + 1)
                        act.activation(h2T[:, 4 * i:4 * i + 4, (t - 1) * P:t * P],
                                       psT[i][:, :].rearrange("p (c j) -> p c j", j=P), ACT.Copy).then_inc(s_h2Tout, 1)
            act.wait_ge(s_logit, 1)
            act.activation(logitsT[0:NG + NE, :], psL[0:NG + NE, :], ACT.Copy).then_inc(s_logitout, 1)
            act.wait_ge(s_gshift, 1)
            act.activation(gexp, gexp, ACT.Exp).then_inc(s_rexp, 1)
            act.wait_ge(s_diff, 1)
            act.activation(ratio, ratio, ACT.Exp).then_inc(s_rexp, 1)

        @block.vector
        def _(dve):
            dve.tensor_tensor(col[:, 0:KC], k.mod[:, 16:24], k.col(C_P1, KC), ALU.mult).then_inc(s_col, 1)
            dve.scalar_tensor_tensor(col[:, KC:2 * KC], k.mod[:, 32:40], 1.0, k.col(C_G2, KC),
                                     ALU.add, ALU.mult).then_inc(s_col, 1)
            dve.tensor_tensor(col[:, 2 * KC:3 * KC], k.mod[:, 40:48], k.col(C_P2, KC), ALU.mult).then_inc(s_col, 1)
            dve.wait_ge(s_col, 3)
            columns = [col[:, 0:KC], col[:, KC:2 * KC], k.mod[:, 24:32], col[:, 2 * KC:3 * KC]]
            for n in range(4 * KC + 4):
                if n < 4 * KC:
                    if n >= 4:
                        dve.wait_ge(s_row, n - 3)
                    dve.tensor_scalar(diag[n % 4], ident, columns[n // KC][:, n % KC:n % KC + 1], None,
                                      ALU.mult).then_inc(s_diag, 1)
                if n % 4 == 3 and n < 4 * KC:
                    dve.wait_ge(s_row, n + 1)
                    half = (n % KC) // 4
                    dve.tensor_copy(rows[n // KC][:, half * 512:(half + 1) * 512], psR[:, :]).then_inc(s_rowout, 1)
            gt1, a2, b2, _ = rows
            dve.wait_ge(s_rowout, KC)
            dve.wait_ge(s_x1in, 16)
            for t in range(TT):
                dve.wait_ge(s_ysq, 2 * t + 2)
                dve.tensor_tensor(rs[:, 0, t:t + 1], ss[:, 0, t:t + 1], ss[:, 1, t:t + 1], ALU.add).then_inc(s_yms, 1)
                dve.wait_ge(s_yms, 3 * t + 1)
                dve.tensor_scalar(rs[:, 0, t:t + 1], rs[:, 0, t:t + 1], 1.0 / D, EPS, ALU.mult, ALU.add).then_inc(s_yms, 1)
                dve.wait_ge(s_yms, 3 * t + 2)
                dve.reciprocal(rs[:, 0, t:t + 1], rs[:, 0, t:t + 1]).then_inc(s_yms, 1)
                dve.wait_ge(s_yroot, t + 1)
                for i in range(2):
                    c = slice(i * 512, (i + 1) * 512)
                    dve.scalar_tensor_tensor(h2[:, t, c], psY[t % 2][i][:, :], rs[:, 0, t:t + 1], gt1[:, c],
                                             ALU.mult, ALU.mult).then_inc(s_yout, 1)
                dve.wait_ge(s_yout, 2 * t + 2)
                dve.tensor_tensor(x1[:, t, :], x1[:, t, :], h2[:, t, :], ALU.add).then_inc(s_x1, 1)
                dve.wait_ge(s_xsq, t + 1)
                dve.tensor_scalar(rs[:, 1, t:t + 1], ss2[:, t:t + 1], 1.0 / D, EPS, ALU.mult, ALU.add).then_inc(s_xms, 1)
                dve.wait_ge(s_xms, 2 * t + 1)
                dve.reciprocal(rs[:, 1, t:t + 1], rs[:, 1, t:t + 1]).then_inc(s_xms, 1)
                dve.wait_ge(s_xroot, t + 1)
                dve.scalar_tensor_tensor(h2[:, t, :], x1[:, t, :], rs[:, 1, t:t + 1], a2, ALU.mult,
                                         ALU.mult).then_inc(s_h2, 1)
                dve.wait_ge(s_h2, 2 * t + 1)
                dve.tensor_tensor(h2[:, t, :], h2[:, t, :], b2, ALU.add).then_inc(s_h2, 1)

            n = 0

            def done(ins):
                nonlocal n
                n += 1
                ins.then_inc(s_r, 1)
                dve.wait_ge(s_r, n)

            def bc(ap, shape):
                return ap.unsqueeze(2).to_broadcast(shape)

            dve.wait_ge(s_logitp, 1)
            done(dve.tensor_tensor(logits, psR[:, 0:TT * 64].rearrange("p (t j) -> p t j", j=64)[:, :, 0:NG + NE],
                                   k.col(C_RB, NG + NE).unsqueeze(1).to_broadcast([P, TT, NG + NE]), ALU.add))
            groups = logits[:, :, 0:NG]
            experts = logits[:, :, NG:NG + NE].rearrange("p t (g e) -> p t g e", e=EG)
            done(dve.tensor_scalar(first, k.const("experts")[:, 0:EG], -1.0, float(EG), ALU.mult, ALU.add))
            done(dve.tensor_reduce(gmax, groups, AX.X, ALU.max))
            dve.tensor_tensor(gexp, groups, bc(gmax, [P, TT, NG]), ALU.subtract).then_inc(s_gshift, 1)

            def argmax(one_hot, values, largest, eq, best, width):
                done(dve.tensor_tensor(eq, values, bc(largest, [P, TT, width]), ALU.is_equal))
                done(dve.tensor_tensor(eq, eq, first[:, 0:width].unsqueeze(1).to_broadcast([P, TT, width]), ALU.mult))
                done(dve.tensor_reduce(best, eq, AX.X, ALU.max))
                done(dve.tensor_tensor(one_hot, eq, bc(best, [P, TT, width]), ALU.is_equal))

            argmax(gone, groups, gmax, geq, gbest, NG)
            done(dve.tensor_tensor(per_group, experts, gone.unsqueeze(3).to_broadcast([P, TT, NG, EG]), ALU.mult))
            done(dve.tensor_reduce(ing, per_group.rearrange("p t g e -> p t e g"), AX.X, ALU.add))
            for i in range(2):
                done(dve.tensor_reduce(top[i], ing, AX.X, ALU.max))
                argmax(one[i], ing, top[i], eq, best, EG)
                done(dve.tensor_tensor(chosen[i].rearrange("p t (g e) -> p t g e", e=EG),
                                       gone.unsqueeze(3).to_broadcast([P, TT, NG, EG]),
                                       one[i].unsqueeze(2).to_broadcast([P, TT, NG, EG]), ALU.mult))
                if i == 0:
                    done(dve.scalar_tensor_tensor(ing, one[0], NEG, ing, ALU.mult, ALU.add))
            dve.tensor_tensor(ratio, top[1], top[0], ALU.subtract).then_inc(s_diff, 1)
            done(dve.tensor_tensor(both, chosen[0], chosen[1], ALU.add))
            dve.tensor_reduce(both_sum, both.rearrange("p t e -> p e t"), AX.X, ALU.add).then_inc(s_both, 1)
            dve.wait_ge(s_rank, 2)
            done(dve.tensor_copy(rank[:, 0, :], psT[0][:, 0:NE]))
            done(dve.tensor_copy(count, psT[1][:, 0:NE]))
            for t in range(1, TT):
                done(dve.tensor_tensor(rank[:, t, :], rank[:, t - 1, :], both[:, t - 1, :], ALU.add))
            done(dve.scalar_tensor_tensor(k.place, rank, 1.0, both, ALU.add, ALU.mult))
            done(dve.tensor_scalar(k.place, k.place, -1.0, None, ALU.add))
            done(dve.tensor_tensor(over, count.unsqueeze(2).to_broadcast([P, NE, T // SL - 1]),
                                   k.const("tiles").unsqueeze(1).to_broadcast([P, NE, T // SL - 1]), ALU.is_gt))
            done(dve.tensor_reduce(tiles, over, AX.X, ALU.add))
            done(dve.tensor_scalar(tiles, tiles, 1.0, None, ALU.add))
            done(dve.tensor_copy(cum[0][:, 0, :], tiles))
            done(dve.tensor_copy(cum[0][:, 1, :], count))
            for i in range(5):
                old, new, d = cum[i % 2], cum[(i + 1) % 2], 2 ** i
                done(dve.tensor_copy(new[:, :, 0:d], old[:, :, 0:d]))
                done(dve.tensor_tensor(new[:, :, d:NE], old[:, :, d:NE], old[:, :, 0:NE - d], ALU.add))
            tiles_upto, tokens_upto = cum[1][:, 0, :], cum[1][:, 1, :]
            done(dve.tensor_copy(k.upto, tiles_upto))
            done(dve.tensor_copy(k.tiles, tiles))
            done(dve.tensor_tensor(before, tokens_upto, count, ALU.subtract))
            done(dve.tensor_tensor(base, rank, before.unsqueeze(1).to_broadcast([P, TT, NE]), ALU.add))
            for i in range(2):
                done(dve.tensor_tensor(chosen[i], chosen[i], base, ALU.mult))
                done(dve.tensor_reduce(rowf[i], chosen[i], AX.X, ALU.add))
                done(dve.tensor_copy(k.row[i], rowf[i]))
            shape = [P, ITEMS_MAX + 1, NE]
            places = k.const("slots")[:, 0:ITEMS_MAX + 1]
            done(dve.tensor_tensor(past, places.unsqueeze(2).to_broadcast(shape),
                                   tiles_upto.unsqueeze(1).to_broadcast(shape), ALU.is_ge))
            done(dve.tensor_reduce(expert, past, AX.X, ALU.add))
            for total, per_expert in ((place, tiles), (row, count)):
                done(dve.tensor_tensor(spare, past, per_expert.unsqueeze(1).to_broadcast(shape), ALU.mult))
                done(dve.tensor_reduce(total, spare, AX.X, ALU.add))
            done(dve.tensor_scalar(expert, expert, float(NE - 1), None, ALU.min))
            done(dve.tensor_tensor(place, places, place, ALU.subtract))
            done(dve.tensor_scalar(place, place, float(SL), float(T - SL), ALU.mult, ALU.min))
            done(dve.tensor_tensor(row, row, place, ALU.add))
            for dst, src in ((k.item_e, expert), (k.item_place, place), (k.item_row, row)):
                done(dve.tensor_copy(dst, src))
            dve.wait_ge(s_rexp, 2)
            done(dve.tensor_reduce(gsum, gexp, AX.X, ALU.add))
            done(dve.tensor_scalar(denom, ratio, 1.0, None, ALU.add))
            done(dve.tensor_tensor(denom, denom, gsum, ALU.mult))
            done(dve.reciprocal(k.weight[0], denom))
            done(dve.tensor_tensor(k.weight[1], k.weight[0], ratio, ALU.mult))


E_SEL = M_HT
E_X = E_SEL + TT * SL
E_XT = E_X + 512
E_SILU = E_XT + 512
E_HE = E_SILU + DE // 2
E_HET = E_HE + DE // 2
E_Y = E_HET + DE // 2


def experts(k):
    nc, dram = k.nc, k.dram
    h2 = k.view(M_H2, TT, D)
    sel = k.view(E_SEL, TT, SL)
    x, silu, he, y = k.view(E_X, 512), k.view(E_SILU, DE // 2), k.view(E_HE, DE // 2), k.view(E_Y, 512)
    xT = k.view(E_XT, 4, 2, SL)
    heT = k.view(E_HET, 2, 2, SL)
    gate_up = [k.view(3 * j * SLOT, 2, KC, DE) for j in range(2)]
    down = [k.view((3 * j + 2) * SLOT, DE // P, D) for j in range(2)]
    ident = k.const("ident")
    psX, psXT, psGU, psHT, psY = k.banks[0:5]

    s_sel, s_x, s_xout = k.sem("s_sel"), k.sem("s_x"), k.sem("s_xout")
    s_xT, s_xTout = k.sem("s_xT"), k.sem("s_xTout")
    s_gu, s_silu, s_he = k.sem("s_gu"), k.sem("s_silu"), k.sem("s_he")
    s_heT, s_heTout = k.sem("s_heT"), k.sem("s_heTout")
    s_down, s_yout, s_store = k.sem("s_down"), k.sem("s_yout"), k.sem("s_store")
    s_end = k.sem("s_end")

    def tiles_of_all(eng):
        return eng.value_load(k.total[0:1, 0:1], min_val=NE, max_val=ITEMS_MAX)

    with nc.Block() as block:
        @block.sync
        def _(sp):
            load_expert(sp, k, 1, 1)
            with sp.Fori(0, NE // 2 - 1) as it:
                for j in range(2):
                    before = sp.value_load(k.upto[0:1, bass.ds(it * 2 + j, 1)], min_val=1, max_val=ITEMS_MAX)
                    sp.wait_ge(s_down, before + START)
                    load_expert(sp, k, it * 2 + (j + 2), j, static=False)

        @block.tensor
        def _(pe):
            pe.sem_inc(s_down, START)
            pe.sem_inc(s_heT, START)
            def gather():
                for t in range(TT):
                    for half in range(2):
                        mm = pe.matmul(psX[half * SL:(half + 1) * SL, :], sel[:, t, :],
                                       h2[:, t, half * 512:(half + 1) * 512], start=(t == 0), stop=(t == TT - 1))
                mm.then_inc(s_x, 1)

            def transpose_x():
                for c in range(4):
                    mm = pe.transpose(psXT[:, c * P:(c + 1) * P], x[:, c * P:(c + 1) * P], ident)
                mm.then_inc(s_xT, 1)

            def tile(w, it, j):
                gate_there, up_there, down_there = k.s_expert[j]
                pe.wait_ge(gate_there, it * 16 + 16)
                pe.wait_ge(up_there, it * 16 + 16)
                pe.wait_ge(s_xTout, w + 1)
                for c in range(KC):
                    for half in range(2):
                        mm = pe.matmul(psGU[half * SL:(half + 1) * SL, :], xT[:, c % 4, c // 4, :],
                                       gate_up[j][:, :, c, half * (DE // 2):(half + 1) * (DE // 2)],
                                       start=(c == 0), stop=(c == KC - 1))
                mm.then_inc(s_gu, 1)
                pe.wait_ge(s_sel, w + 2)
                gather()
                pe.wait_ge(s_he, w + 1 + START)
                for c in range(2):
                    mm = pe.transpose(psHT[:, c * P:(c + 1) * P], he[:, c * P:(c + 1) * P], ident)
                mm.then_inc(s_heT, 1)
                pe.wait_ge(s_xout, w + 2)
                transpose_x()
                pe.wait_ge(down_there, it * 16 + 16)
                pe.wait_ge(s_heTout, w + 1)
                pe.wait_ge(s_yout, w + START)
                for c in range(DE // P):
                    for half in range(2):
                        mm = pe.matmul(psY[half * SL:(half + 1) * SL, :], heT[:, c % 2, c // 2, :],
                                       down[j][:, c, half * 512:(half + 1) * 512],
                                       start=(c == 0), stop=(c == DE // P - 1))
                mm.then_inc(s_down, 1)

            pe.wait_ge(s_sel, 1)
            gather()
            pe.wait_ge(s_xout, 1)
            transpose_x()
            done = pe.alloc_register("tiles_done")
            pe.reg_mov(done, 0)
            with pe.Fori(0, NE // 2) as it:
                for j in range(2):
                    tiles = pe.value_load(k.tiles[0:1, bass.ds(it * 2 + j, 1)], min_val=1, max_val=T // SL)
                    with pe.Fori(0, tiles) as _t:
                        tile(pe.snap(done, min_val=0, max_val=ITEMS_MAX), it, j)
                        pe.reg_add(done, done, 1)

        @block.scalar
        def _(act):
            act.sem_inc(s_store, START)
            total = tiles_of_all(act)
            act.wait_ge(s_x, 1)
            act.activation(x, psX[:, :], ACT.Copy).then_inc(s_xout, 1)
            with act.Fori(0, total) as w:
                row = act.value_load(k.item_row[0:1, bass.ds(w, 1)], min_val=0, max_val=ROWS_OUT)
                act.wait_ge(s_gu, w + 1)
                act.wait_ge(s_he, w + START)
                act.activation(silu, psGU[:, 0:DE // 2], ACT.Silu).then_inc(s_silu, 1)
                act.wait_ge(s_x, w + 2)
                act.wait_ge(s_xT, w + 1)
                act.activation(x, psX[:, :], ACT.Copy).then_inc(s_xout, 1)
                act.wait_ge(s_heT, w + 1 + START)
                act.wait_ge(s_down, w + START)
                act.activation(heT.rearrange("p a b c -> p (a b c)"), psHT[:, 0:2 * P], ACT.Copy).then_inc(s_heTout, 1)
                act.wait_ge(s_yout, w + 1 + START)
                act.dma_start(dram["rows"][bass.ds(row, SL), :].rearrange("r (h n) -> h r n", h=2),
                              y).then_inc(s_store, 16)
            act.wait_ge(s_store, total * 16 + START)
            act.sem_inc(s_end, 1)

        @block.vector
        def _(dve):
            dve.sem_inc(s_he, START)
            dve.sem_inc(s_yout, START)
            def select(w):
                e = dve.value_load(k.item_e[0:1, bass.ds(w, 1)], min_val=0, max_val=NE - 1)
                t = dve.value_load(k.item_place[0:1, bass.ds(w, 1)], min_val=0, max_val=T - SL)
                return (k.const("slots")[:, bass.ds(t, SL)].unsqueeze(1).to_broadcast([P, TT, SL]),
                        k.place[:, :, bass.ds(e, 1)].to_broadcast([P, TT, SL]))

            total = tiles_of_all(dve)
            places, place = select(0)
            dve.tensor_tensor(sel, places, place, ALU.is_equal).then_inc(s_sel, 1)
            dve.wait_ge(s_xT, 1)
            dve.tensor_copy(xT.rearrange("p a b c -> p (a b c)"), psXT[:, :]).then_inc(s_xTout, 1)
            with dve.Fori(0, total) as w:
                places, place = select(w + 1)
                dve.wait_ge(s_x, w + 1)
                dve.tensor_tensor(sel, places, place, ALU.is_equal).then_inc(s_sel, 1)
                dve.wait_ge(s_silu, w + 1)
                dve.wait_ge(s_heT, w + START)
                dve.tensor_tensor(he, silu, psGU[:, DE // 2:DE], ALU.mult).then_inc(s_he, 1)
                dve.wait_ge(s_xT, w + 2)
                dve.wait_ge(s_gu, w + 1)
                dve.tensor_copy(xT.rearrange("p a b c -> p (a b c)"), psXT[:, :]).then_inc(s_xTout, 1)
                dve.wait_ge(s_down, w + 1 + START)
                dve.wait_ge(s_store, w * 16 + START)
                dve.tensor_copy(y, psY[:, :]).then_inc(s_yout, 1)


def finish(k):
    nc, dram = k.nc, k.dram
    x1 = k.view(M_X1, TT, D)
    gt2 = k.view(M_GT2, D)
    picked = k.view(0, 2, TT, D)
    total = k.view(2 * TT * D, TT, D)
    junk = k.view(3 * TT * D, D)
    ms, rstd = k.misc(TT), k.misc(TT)
    s_gather = [k.sem(f"s_gather{t}") for t in range(TT)]
    s_sum = k.sem("s_sum")
    s_sq = k.sem("s_sq")
    s_ms = k.sem("s_ms")
    s_root = k.sem("s_root")
    s_out = k.sem("s_out")
    s_stored = k.sem("s_stored")

    with nc.Block() as block:
        @block.gpsimd
        def _(pool):
            for t in range(TT):
                for i in range(2):
                    pool.indirect_dma_start(picked[:, i, t, :], None, dram["rows"][0:ROWS_OUT, :],
                                            bass.IndirectOffsetOnAxis(ap=k.row[i][:, t:t + 1], axis=0)
                                            ).then_inc(s_gather[t], 16)

        @block.vector
        def _(dve):
            for t in range(TT):
                dve.wait_ge(s_gather[t], 32)
                dve.tensor_scalar(total[:, t, :], picked[:, 0, t, :], k.weight[0][:, t:t + 1], None,
                                  ALU.mult).then_inc(s_sum, 1)
                dve.wait_ge(s_sum, 2 * t + 1)
                dve.scalar_tensor_tensor(total[:, t, :], picked[:, 1, t, :], k.weight[1][:, t:t + 1], total[:, t, :],
                                         ALU.mult, ALU.add).then_inc(s_sum, 1)
                dve.wait_ge(s_sq, t + 1)
                dve.tensor_scalar(rstd[:, t:t + 1], ms[:, t:t + 1], 1.0 / D, EPS, ALU.mult, ALU.add).then_inc(s_ms, 1)
                dve.wait_ge(s_ms, 2 * t + 1)
                dve.reciprocal(rstd[:, t:t + 1], rstd[:, t:t + 1]).then_inc(s_ms, 1)
                dve.wait_ge(s_root, t + 1)
                dve.scalar_tensor_tensor(total[:, t, :], total[:, t, :], rstd[:, t:t + 1], gt2, ALU.mult,
                                         ALU.mult).then_inc(s_out, 1)
                dve.wait_ge(s_out, 2 * t + 1)
                dve.tensor_tensor(total[:, t, :], total[:, t, :], x1[:, t, :], ALU.add).then_inc(s_out, 1)

        @block.scalar
        def _(act):
            for t in range(TT):
                act.wait_ge(s_sum, 2 * t + 2)
                if t:
                    act.wait_ge(s_sq, t)
                act.activation(junk, total[:, t, :], ACT.Square, accum_out=ms[:, t:t + 1]).then_inc(s_sq, 1)
                act.wait_ge(s_ms, 2 * t + 2)
                act.activation(rstd[:, t:t + 1], rstd[:, t:t + 1], ACT.Sqrt).then_inc(s_root, 1)

        @block.sync
        def _(sp):
            for t in range(TT):
                sp.wait_ge(s_out, 2 * t + 2)
                sp.dma_start(dram["out"][t * P:(t + 1) * P, :], total[:, t, :]).then_inc(s_stored, 16)
            sp.wait_ge(s_stored, 16 * TT)


def layout(i):
    a = {n: np.asarray(v) for n, v in i.items()}

    def cols(v):
        return v.reshape(-1, P).T

    def rows(v):
        return np.broadcast_to(v[None, :], (P, v.size))

    w_conv = a["w_conv_dn"][0]
    parts = [cols(a["b_ada"][0]), cols(a["g_pre_mix"][0]), cols(a["g_post_mix"][0]), cols(a["g_pre_ffn"][0]),
             cols(a["g_post_ffn"][0]), cols(a["c"][0]),
             w_conv.reshape(CONV, 3 * FC, P).transpose(2, 1, 0).reshape(P, -1),
             np.concatenate([a["g_onorm_dn"][0]] * 2)[:, None],
             np.repeat(a["a_log_dn"][0], CH, axis=0), np.repeat(a["dt_bias_dn"][0], CH, axis=0),
             rows(a["b_group"][0]), rows(a["b_expert"][0])]
    rpb = np.pad(a["rpb_na"][0], ((0, 0), (0, 0), (16, 17)))
    r, c = np.divmod(np.arange(P), WIN)
    bias = rpb[:, (7 - r)[:, None, None] + np.arange(ROWS)[None, :, None],
               (15 - c)[:, None, None] + np.arange(QB)[None, None, :]].transpose(1, 0, 2, 3)
    cs = constants()
    return {
        "x": a["x"][0], "cols": np.concatenate(parts, axis=1), "consts": np.concatenate([cs[n] for n in CONST], axis=1),
        "w_ada": a["w_ada"][0], "w_in": a["w_in"][0], "w_out": a["w_out"][0], "bias": bias.reshape(P, -1),
        "w_route": np.concatenate([a["w_group"][0], a["w_expert"][0]], axis=1),
        "w_gate": a["w_gate"][0], "w_up": a["w_up"][0], "w_down": a["w_down"][0],
    }


STAGES = [project, attend, delta, route, experts, finish]


def build(nc, dram, stages):
    with ExitStack() as ctx:
        k = Kernel(nc, ctx, dram)
        for stage in stages:
            k.stage = stage.__name__
            stage(k)
            k.end_stage()


def kernel(**inputs):
    import concourse.bacc as bacc
    from concourse.bass_utils import run_bass_kernel_spmd

    nc = bacc.Bacc("TRN2", target_bir_lowering=False, num_devices=1)
    arrays = {n: np.ascontiguousarray(v) for n, v in layout(inputs).items()}
    dram = {n: nc.dram_tensor(f"in_{n}", v.shape, mybir.dt.from_np(v.dtype), kind="ExternalInput").ap()
            for n, v in arrays.items()}
    dram["out"] = nc.dram_tensor("out", (T, D), F32, kind="ExternalOutput").ap()
    dram["rows"] = nc.dram_tensor("rows", (ROWS_OUT + SL, D), F32, kind="Internal").ap()
    build(nc, dram, STAGES)
    r = run_bass_kernel_spmd(nc, [{f"in_{n}": v for n, v in arrays.items()}], core_ids=[0])
    return r.results[0]["out"].reshape(1, T, D)
```

```python
from contextlib import ExitStack

import numpy as np

import concourse.bass as bass
from concourse import mybir

F32 = mybir.dt.float32
F32R = mybir.dt.float32r
I32 = mybir.dt.int32
U32 = mybir.dt.uint32
ALU = mybir.AluOpType
ACT = mybir.ActivationFunctionType
AX = mybir.AxisListType

P = 128
T = 512
D = 1024
TT = T // P
KC = D // P
HD = 64
NH = 8
HW = NH * HD
FC = HW // P
CH = 64
STEPS = T // CH
CONV = 5
PAD = CONV // 2
GRID_W, ROWS, WIN = 64, 8, 16
KB = 8
WC = 32
QB = 48
NG, EG, NE = 4, 8, 32
DE = 512
SL = 64
LEVELS = 6
EPS = 1e-6
NEG = -1e30

C_BADA, C_G1, C_P1, C_G2, C_P2, C_C = 0, 48, 56, 64, 72, 80
C_CONV, C_ONORM, C_ALOG, C_DT, C_RB = 88, 148, 149, 157, 165
NCOL = C_RB + NG + NE


def constants():
    i = np.arange(P)
    ci = i % CH
    half = i // CH
    same = half[:, None] == half[None, :]
    fwd = (half == 0)[:, None]
    r, c = ci[:, None], ci[None, :]
    j = np.arange(CH)[None, :]
    out = {
        "ident": np.eye(P),
        "fold": np.concatenate([np.eye(CH)] * 2),
        "after": same * np.where(fwd, r > c, r < c),
        "upto": same * np.where(fwd, r <= c, r >= c),
        "uptoc": np.where(half[:, None] == 0, r <= j, r >= j),
        "halves": same * 1.0,
    }
    levels = []
    for s in range(LEVELS):
        b = 2 ** s
        pair = (r // (2 * b)) == (j // (2 * b))
        f = pair & ((j // b) % 2 == 1) & ((r // b) % 2 == 0)
        g = pair & ((j // b) % 2 == 0) & ((r // b) % 2 == 1)
        levels.append(np.where(half[:, None] == 0, f, g))
    out["levels"] = np.stack(levels, 1).reshape(P, LEVELS * CH)
    q = i % WIN
    masks = []
    for delta, base in ((0, 0), (-8, 16), (-16, 48)):
        col = base + q
        c0 = np.clip(col - WIN // 2, 0, GRID_W - WIN)
        k = base + delta + np.arange(WC)
        ok = (k[None, :] >= c0[:, None]) & (k[None, :] < c0[:, None] + WIN)
        masks.append(np.where(ok, 0.0, NEG))
    out["window"] = np.stack(masks, 1).reshape(P, 3 * WC)
    out["slots"] = np.broadcast_to(np.arange(T)[None, :], (P, T))
    out["experts"] = np.broadcast_to(np.arange(NE)[None, :], (P, NE))
    out["before"] = (i[:, None] < i[None, :]) * 1.0
    out["ones"] = np.ones((P, P))
    out["tiles"] = np.broadcast_to(np.arange(1, T // SL)[None, :] * SL, (P, T // SL - 1))
    return {k: np.ascontiguousarray(v, dtype=np.float32) for k, v in out.items()}


CONST = {}
_at = 0
for _k, _w in (("ident", P), ("fold", CH), ("after", P), ("upto", P), ("uptoc", CH), ("halves", P),
               ("levels", LEVELS * CH), ("window", 3 * WC), ("slots", T), ("experts", NE), 
               ("before", P), ("ones", P), ("tiles", T // SL - 1)):
    CONST[_k] = (_at, _w)
    _at += _w
NCONST = _at

SLOT = 4096
NSLOT = 6
M_HT = NSLOT * SLOT
M_QKV = M_HT + KC * T
M_Z = M_QKV + 3 * FC * T
M_MIX = M_Z + FC * T
M_NA = M_MIX + 2 * FC * T
M_C = M_NA + 3 * FC * T
M_COL = M_C + NCONST
M_WAB = M_COL + NCOL
M_MISC = M_WAB + KC * (NG + NE)
MEM = M_MISC + 3000


class Kernel:

    def __init__(self, nc, ctx, dram):
        self.nc, self.ctx, self.dram = nc, ctx, dram
        self.upper = ctx.enter_context(nc.sbuf_tensor("upper", [P, MEM - SPLIT], F32))
        self.gate_parts = ctx.enter_context(nc.sbuf_tensor("gate_parts", [P, 2 * KC * 4 * NH], F32R))
        self.lower = None
        self.banks = [ctx.enter_context(nc.psum_tensor(f"bank{i}", [P, 512], F32)) for i in range(8)]
        self.misc_at = M_MISC
        self.local = []
        self.stage = "all"
        self.mod = self.misc(48)
        self.g = self.misc(STEPS, NH)
        self.beta = self.misc(STEPS, NH)
        self.s_const = self.sem("s_const")
        self.s_cols = self.sem("s_cols")
        self.s_bias = self.sem("s_bias")
        self.s_expert = [[self.sem(f"s_{w}{j}") for w in ("gate", "up", "down")] for j in range(3)]
        self.s_w_out = [self.sem("s_w_out_dn"), self.sem("s_w_out_na")]
        self.s_w_route = self.sem("s_w_route")
        self.free_misc = self.misc_at
        self.local = []

    def sem(self, name):
        s = self.nc.alloc_semaphore(name=f"{self.stage}_{name}")
        self.local.append(s)
        return s

    def end_stage(self):
        self.nc.clear_and_free_semaphores(self.local)
        self.nc.all_engine_barrier()
        self.local = []

    def between(self, start, end):
        if start >= SPLIT:
            return self.upper[:, start - SPLIT:end - SPLIT]
        assert end <= SPLIT
        return self.lower[:, start:end]

    def view(self, at, *shape):
        n = int(np.prod(shape))
        v = self.between(at, at + n)
        if len(shape) == 2:
            return v.rearrange("p (a b) -> p a b", b=shape[1])
        if len(shape) == 3:
            return v.rearrange("p (a b c) -> p a b c", b=shape[1], c=shape[2])
        if len(shape) == 4:
            return v.rearrange("p (a b c d) -> p a b c d", b=shape[1], c=shape[2], d=shape[3])
        return v

    def misc(self, *shape):
        at = self.misc_at
        self.misc_at += int(np.prod(shape))
        assert self.misc_at <= MEM
        return self.view(at, *shape)

    def const(self, name):
        at, w = CONST[name]
        return self.between(M_C + at, M_C + at + w)

    def col(self, at, n=1):
        return self.between(M_COL + at, M_COL + at + n)


SPLIT = 4 * SLOT
RING_SLOTS = 3
RING_AT = SPLIT

ITEMS = [("ada", 0), ("ada", 1), ("ada", 2), ("ada", 3), ("in", 0), ("ada", 4), ("in", 1), ("ada", 5), ("in", 2),
         ("ada", 6), ("in", 3), ("ada", 7), ("in", 4), ("ada", 8), ("ada", 9), ("in", 5), ("ada", 10), ("ada", 11),
         ("in", 6)]
IN_AT = [0, HW, 2 * HW, 3 * HW, 4 * HW + 4 * NH, 5 * HW + 4 * NH, 6 * HW + 4 * NH]


def ada_before(b):
    n = ITEMS.index(("in", b))
    m = n
    while ITEMS[m - 1][0] == "ada" and m > 4:
        m -= 1
    return [a for _, a in ITEMS[m:n]]


def items_done(eng, k, n):
    ada = sum(kind == "ada" for kind, _ in ITEMS[:n])
    if ITEMS[n - 1][0] == "ada":
        eng.wait_ge(k.s_ada, ada)
    else:
        eng.wait_ge(k.s_split, FC * (n - ada))


def project(k):
    nc, dram = k.nc, k.dram
    qkv = k.view(M_QKV, 3 * FC, T)
    zT = k.view(M_Z, FC, T)
    na = k.view(M_NA, 3 * FC, T)
    x_sb = k.view(M_NA, TT, D)
    padded = [k.between(M_MIX + i * 520, M_MIX + i * 520 + T + 2 * PAD) for i in range(2)]
    conv = [k.between(M_MIX + 1040 + i * T, M_MIX + 1040 + (i + 1) * T) for i in range(2)]
    square = [k.between(M_MIX + 2064 + i * T, M_MIX + 2064 + (i + 1) * T) for i in range(2)]
    inv = k.between(M_MIX + 3088, M_MIX + 3088 + T)
    w_ab = k.view(M_WAB, KC, 4 * NH)
    abT = k.misc(T)
    hT = [k.between(M_QKV + D + i * T, M_QKV + D + (i + 1) * T) for i in range(4)]
    parts = k.parts.rearrange("p (a b) -> p a b", b=SLOT)
    w_high, w_low = ([parts[:, j, i * KC * P:(i + 1) * KC * P].rearrange("p (c m) -> p c m", m=P) for i in range(4)]
                     for j in range(2))
    h_high, h_low = (parts[:, j, :].rearrange("p (c t) -> p c t", t=T) for j in range(2, 4))
    ab_high, ab_low = (k.gate_parts[:, i * KC * 4 * NH:(i + 1) * KC * 4 * NH].rearrange("p (c m) -> p c m", m=4 * NH)
                       for i in range(2))
    junk = k.between(M_QKV, M_QKV + D)
    ident = k.const("ident")
    amod, cond, stat, rstd = k.misc(KC), k.misc(KC), k.misc(TT), k.misc(TT)
    ga, gabs, gb = (k.misc(STEPS * NH).rearrange("p (s h) -> p s h", h=NH) for _ in range(3))
    expa = k.misc(NH)
    condpad = k.view(M_MIX + 3600, KC, 32)
    partial = [k.between(M_NA + TT * D + i * 512, M_NA + TT * D + (i + 1) * 512) for i in range(2)]

    s_x = k.sem("s_x")
    s_ab_w = k.sem("s_ab_w")
    s_slot = [k.sem(f"s_slot{i}") for i in range(RING_SLOTS)]
    k.s_ada = k.sem("s_ada")
    k.s_tile = k.sem("s_tile")
    s_cond = k.sem("s_cond")
    s_high = k.sem("s_high")
    k.s_split = k.sem("s_split")
    s_abhigh = k.sem("s_abhigh")
    s_hhigh = k.sem("s_hhigh")
    s_hsplit = k.sem("s_hsplit")
    s_abT = k.sem("s_abT")
    s_condpad = k.sem("s_condpad")
    s_condzero = k.sem("s_condzero")
    s_arow = k.sem("s_arow")
    s_acol = k.sem("s_acol")
    s_ared = k.sem("s_ared")
    s_abias = k.sem("s_abias")
    s_mod = k.sem("s_mod")
    s_stat = k.sem("s_stat")
    s_rstd = k.sem("s_rstd")
    s_xn = k.sem("s_xn")
    s_xT = k.sem("s_xT")
    s_hT = k.sem("s_hT")
    s_evac = k.sem("s_evac")
    s_evacv = k.sem("s_evacv")
    s_pad = k.sem("s_pad")
    s_tap = k.sem("s_tap")
    s_silu = k.sem("s_silu")
    s_sq = k.sem("s_sq")
    s_ident = k.sem("s_ident")
    s_ss = k.sem("s_ss")
    s_inv = k.sem("s_inv")
    s_root = k.sem("s_root")
    k.s_norm = k.sem("s_norm")
    s_ab = k.sem("s_ab")
    s_gate = k.sem("s_gate")
    s_gact = k.sem("s_gact")

    NT = 7 * FC
    NDN = 3 * FC
    psA = [k.banks[0], k.banks[1]]
    RING = 4
    psP = k.banks[2:6]
    psS = k.banks[6]
    psG = k.banks[7]

    by_act = [f < 20 for f in range(NT)]
    acts = [sum(by_act[:f + 1]) for f in range(NT)]
    dves = [f + 1 - acts[f] for f in range(NT)]

    def weights_of(f):
        n = ITEMS.index(("in", f // FC))
        return k.view(RING_AT + (n % RING_SLOTS) * SLOT, KC, 512)[:, :, (f % FC) * P:(f % FC + 1) * P]

    with nc.Block() as block:
        @block.sync
        def _(sp):
            sp.dma_start(k.between(M_COL, M_COL + NCOL), dram["cols"]).then_inc(k.s_cols, 16)
            sp.dma_start(ident, dram["consts"][:, 0:P]).then_inc(s_ident, 16)
            sp.dma_start(x_sb, dram["x"].rearrange("(t p) d -> p t d", p=P)).then_inc(s_x, 16)
            for n, (kind, b) in enumerate(ITEMS):
                if n >= RING_SLOTS:
                    items_done(sp, k, n - RING_SLOTS + 1)
                at = b * 512 if kind == "ada" else IN_AT[b]
                src = dram["w_ada" if kind == "ada" else "w_in"][:, at:at + 512]
                sp.dma_start(k.view(RING_AT + (n % RING_SLOTS) * SLOT, KC, 512),
                             src.rearrange("(c p) n -> p c n", p=P)).then_inc(s_slot[n % RING_SLOTS], 16)
                if n == 4:
                    sp.dma_start(k.between(M_C + P, M_C + NCONST), dram["consts"][:, P:NCONST]).then_inc(k.s_const, 16)
                    sp.dma_start(w_ab, dram["w_in"][:, 4 * HW:4 * HW + 4 * NH].rearrange("(c p) n -> p c n", p=P)
                                 ).then_inc(s_ab_w, 16)
            n = len(ITEMS) - 2
            assert RING_AT + (n % RING_SLOTS) * SLOT == A_BIAS
            items_done(sp, k, n + 1)
            sp.dma_start(k.between(A_BIAS, A_BIAS + NH * ROWS * QB), dram["bias"]).then_inc(k.s_bias, 16)

        @block.gpsimd
        def _(pool):
            for i in range(2):
                pool.memset(padded[i][:, 0:PAD], 0.0).then_inc(s_pad, 1)
                pool.memset(padded[i][:, PAD + T:PAD + T + PAD], 0.0).then_inc(s_pad, 1)

            for f in range(NT):
                pool.wait_ge(s_high, f + 1)
                pool.tensor_tensor(w_low[f % 4], weights_of(f), w_high[f % 4], ALU.subtract).then_inc(k.s_split, 1)
                if f == 2:
                    pool.wait_ge(s_abhigh, 1)
                    pool.tensor_tensor(ab_low, w_ab, ab_high, ALU.subtract).then_inc(s_abhigh, 1)

        @block.tensor
        def _(pe):
            def ada(a, w):
                if a >= 2:
                    pe.wait_ge(s_ared, a - 1)
                for c in range(KC):
                    j = c % 4
                    mm = pe.matmul(psA[a % 2][32 * j:32 * (j + 1), :], condpad[:, c, :], w[:, c, :],
                                   start=(c < 4), stop=(c >= 4))
                mm.then_inc(k.s_ada, 1)

            def ada_columns(a):
                pe.wait_ge(s_arow, a + 1)
                for m in range(4):
                    mm = pe.transpose(psA[a % 2][:, m * P:(m + 1) * P], partial[a % 2][:, m * P:(m + 1) * P], ident)
                mm.then_inc(s_acol, 1)

            def product(out, high, low, c):
                for i, (left, right) in enumerate(((high, h_high), (high, h_low), (low, h_high))):
                    mm = pe.matmul(out, left, right[:, c, :],
                                   start=(c == 0 and i == 0), stop=(c == KC - 1 and i == 2))
                return mm

            tile = 0
            pe.wait_ge(s_condpad, 1)
            pe.wait_ge(s_ident, 16)
            for n, (kind, b) in enumerate(ITEMS):
                w = k.view(RING_AT + (n % RING_SLOTS) * SLOT, KC, 512)
                if kind == "in" and b == 0:
                    for c in range(KC):
                        if c >= 6:
                            pe.wait_ge(s_hT, c - 5)
                        for t in range(TT):
                            if c == 0:
                                pe.wait_ge(s_xn, t + 1)
                            mm = pe.transpose(k.banks[2 + c % 6][:, t * P:(t + 1) * P],
                                              x_sb[:, t, c * P:(c + 1) * P], ident)
                        mm.then_inc(s_xT, 1)
                    pe.wait_ge(s_hT, KC)
                pe.wait_ge(s_slot[n % RING_SLOTS], 16 * (n // RING_SLOTS + 1))
                if kind == "ada":
                    ada(b, w)
                    if 1 <= b < 4:
                        ada_columns(b - 1)
                    if b == 3:
                        ada_columns(b)
                    continue
                for m in range(FC):
                    if tile >= RING:
                        f = tile - RING
                        if by_act[f]:
                            pe.wait_ge(s_evac, acts[f])
                        else:
                            pe.wait_ge(s_evacv, dves[f])
                    pe.wait_ge(k.s_split, tile + 1)
                    for c in range(KC):
                        if tile == 0:
                            pe.wait_ge(s_hsplit, c + 1)
                        mm = product(psP[tile % RING][:, :], w_high[tile % 4][:, c, :], w_low[tile % 4][:, c, :], c)
                    mm.then_inc(k.s_tile, 1)
                    g = tile - NDN - 2 * FC
                    if g >= 0:
                        pe.wait_ge(s_sq, g + 1)
                        if g:
                            pe.wait_ge(s_inv, 2 * g - 1)
                        pe.matmul(psS[:, :], k.const("halves"), square[g % 2], start=True, stop=True).then_inc(s_ss, 1)
                    tile += 1
                    if m == 0:
                        for a in ada_before(b):
                            ada_columns(a)
                if b == 0:
                    pe.wait_ge(k.s_const, 16)
                    pe.wait_ge(s_abhigh, 2)
                    for c in range(KC):
                        mm = product(psG[0:4 * NH, :], ab_high[:, c, :], ab_low[:, c, :], c)
                    mm.then_inc(s_ab, 1)
                if b == 1:
                    pe.wait_ge(s_abT, 1)
                    for s in range(STEPS):
                        for half, chunk in ((0, s), (1, STEPS - 1 - s)):
                            mm = pe.matmul(psG[half * CH:(half + 1) * CH, s * 32:(s + 1) * 32],
                                           abT[0:4 * NH, chunk * CH:(chunk + 1) * CH], ident[0:4 * NH, 0:4 * NH],
                                           start=True, stop=True)
                    mm.then_inc(s_ab, 1)

        @block.scalar
        def _(act):
            act.wait_ge(k.s_cols, 16)
            def ada_rows(a):
                act.wait_ge(k.s_ada, a + 1)
                if a >= 2:
                    act.wait_ge(s_acol, a - 1)
                act.activation(partial[a % 2], psA[a % 2][:, :], ACT.Copy).then_inc(s_arow, 1)

            act.activation(cond, k.col(C_C, KC), ACT.Silu).then_inc(s_cond, 1)
            act.wait_ge(s_x, 16)
            for t in range(TT):
                if t:
                    act.wait_ge(s_stat, t)
                act.activation(junk, x_sb[:, t, :], ACT.Square, accum_out=stat[:, t:t + 1]).then_inc(s_stat, 1)
            act.wait_ge(s_rstd, 2)
            act.activation(rstd, rstd, ACT.Sqrt).then_inc(s_rstd, 1)
            for a in range(4):
                ada_rows(a)
            act.wait_ge(s_mod, 1)
            for c in range(KC):
                act.wait_ge(s_xT, c + 1)
                if c >= 4:
                    act.wait_ge(s_hsplit, c - 3)
                act.activation(hT[c % 4], k.banks[2 + c % 6][:, :], ACT.Identity, bias=k.mod[:, c:c + 1],
                               scale=amod[:, c:c + 1]).then_inc(s_hT, 1)

            act.wait_ge(s_pad, 4)
            for f in range(NDN + 1):
                if f % FC == 0:
                    for a in ada_before(f // FC):
                        ada_rows(a)
                if f < NDN:
                    act.wait_ge(k.s_tile, f + 1)
                    if f >= 2:
                        act.wait_ge(s_tap, CONV * (f - 1))
                    act.activation(padded[f % 2][:, PAD:PAD + T], psP[f % RING][:, :], ACT.Copy).then_inc(s_evac, 1)
                if f == 4:
                    act.wait_ge(s_ab, 1)
                    act.activation(abT[0:4 * NH, :], psG[0:4 * NH, :], ACT.Copy).then_inc(s_abT, 1)
                if f >= 1:
                    act.wait_ge(s_tap, CONV * f)
                    act.activation(qkv[:, f - 1, :], conv[(f - 1) % 2], ACT.Silu).then_inc(s_silu, 1)
            for f in range(NDN, NDN + FC):
                act.wait_ge(k.s_tile, f + 1)
                act.activation(zT[:, f - NDN, :], psP[f % RING][:, :], ACT.Silu).then_inc(s_evac, 1)
            act.wait_ge(s_gate, 7)
            act.activation(gabs, gabs, ACT.Exp, scale=-1.0).then_inc(s_gact, 1)
            act.activation(gb, gb, ACT.Exp, scale=-1.0).then_inc(s_gact, 1)
            act.activation(expa, k.col(C_ALOG, NH), ACT.Exp).then_inc(s_gact, 1)
            act.wait_ge(s_gact, 3)
            act.activation(gabs, gabs, ACT.Ln, bias=1.0).then_inc(s_gact, 1)
            for f in range(NDN + FC, NDN + 2 * FC):
                if f % FC == 0:
                    for a in ada_before(f // FC):
                        ada_rows(a)
                act.wait_ge(k.s_tile, f + 1)
                act.activation(na[:, f - NDN - FC, :].rearrange("p (i r c) -> p r i c", r=ROWS, c=WIN),
                               psP[f % RING][:, :].rearrange("p (r i c) -> p r i c", r=ROWS, c=WIN),
                               ACT.Copy, scale=HD ** -0.5).then_inc(s_evac, 1)
                g = f - NDN - FC
                if g < 2:
                    act.wait_ge(s_silu, g + 1)
                    act.activation(square[g % 2], qkv[:, g, :], ACT.Square).then_inc(s_sq, 1)
            for g in range(2 * FC):
                if g % FC == 0:
                    for a in ada_before((NDN + 2 * FC + g) // FC):
                        ada_rows(a)
                act.wait_ge(s_inv, 2 * g + 2)
                if g:
                    act.wait_ge(k.s_norm, g)
                act.activation(inv, inv, ACT.Sqrt).then_inc(s_root, 1)
                if g + 2 < 2 * FC:
                    act.wait_ge(s_ss, g + 1)
                    act.activation(square[g % 2], qkv[:, g + 2, :], ACT.Square).then_inc(s_sq, 1)

        @block.vector
        def _(dve):
            def ada_sum(a):
                dve.wait_ge(s_acol, a + 1)
                out = k.mod[:, 4 * a:4 * a + 4]
                parts = psA[a % 2][:, :].rearrange("p (m j r) -> p m j r", m=4, r=32)[:, :, :, 0]
                dve.tensor_reduce(out, parts, AX.X, ALU.add).then_inc(s_ared, 1)
                dve.wait_ge(s_ared, a + 1)
                dve.tensor_tensor(out, out, k.col(C_BADA + 4 * a, 4), ALU.add).then_inc(s_abias, 1)

            def high_part(f):
                n = ITEMS.index(("in", f // FC))
                dve.wait_ge(s_slot[n % RING_SLOTS], 16 * (n // RING_SLOTS + 1))
                if f >= 4:
                    dve.wait_ge(k.s_tile, f - 3)
                dve.tensor_copy(w_high[f % 4], weights_of(f)).then_inc(s_high, 1)

            dve.memset(condpad, 0.0).then_inc(s_condzero, 1)
            dve.wait_ge(s_condzero, 1)
            dve.wait_ge(s_cond, 1)
            dve.tensor_copy(condpad[:, :, 0], cond).then_inc(s_condpad, 1)
            dve.wait_ge(s_stat, TT)
            dve.tensor_scalar(rstd, stat, 1.0 / D, EPS, ALU.mult, ALU.add).then_inc(s_rstd, 1)
            dve.wait_ge(s_rstd, 1)
            dve.reciprocal(rstd, rstd).then_inc(s_rstd, 1)
            dve.wait_ge(s_rstd, 3)
            for t in range(TT):
                dve.tensor_scalar(x_sb[:, t, :], x_sb[:, t, :], rstd[:, t:t + 1], None, ALU.mult).then_inc(s_xn, 1)
            for a in range(4):
                ada_sum(a)
            dve.wait_ge(s_abias, 4)
            dve.scalar_tensor_tensor(amod, k.mod[:, 8:16], 1.0, k.col(C_G1, KC), ALU.add, ALU.mult).then_inc(s_mod, 1)
            for f in range(2):
                high_part(f)
            for c in range(KC + 1):
                if c < KC:
                    dve.wait_ge(s_hT, c + 1)
                    dve.tensor_copy(h_high[:, c, :], hT[c % 4]).then_inc(s_hhigh, 1)
                if c >= 1:
                    dve.wait_ge(s_hhigh, c)
                    dve.tensor_tensor(h_low[:, c - 1, :], hT[(c - 1) % 4], h_high[:, c - 1, :],
                                      ALU.subtract).then_inc(s_hsplit, 1)
            for f in range(2, 4):
                high_part(f)
            dve.wait_ge(s_ab_w, 16)
            dve.tensor_copy(ab_high, w_ab).then_inc(s_abhigh, 1)
            for f in range(NDN):
                if f % FC == 2:
                    for a in ada_before(f // FC):
                        ada_sum(a)
                high_part(f + 4)
                dve.wait_ge(s_evac, f + 1)
                if f >= 2:
                    dve.wait_ge(s_silu, f - 1)
                src, dst = padded[f % 2], conv[f % 2]
                for t in range(CONV):
                    w = k.col(C_CONV + f * CONV + t)
                    if t == 0:
                        ins = dve.tensor_scalar(dst, src[:, 0:T], w, None, ALU.mult)
                    else:
                        dve.wait_ge(s_tap, CONV * f + t)
                        ins = dve.scalar_tensor_tensor(dst, src[:, t:t + T], w, dst, ALU.mult, ALU.add)
                    ins.then_inc(s_tap, 1)
                if f == 6:
                    dve.wait_ge(s_ab, 2)
                    ab = psG[:, 0:STEPS * 32].rearrange("p (s g) -> p s g", g=32)
                    for half in range(2):
                        rows = slice(half * CH, (half + 1) * CH)
                        dt = k.col(C_DT, NH)[rows].unsqueeze(1).to_broadcast([CH, STEPS, NH])
                        dve.tensor_tensor(ga[rows], ab[rows, :, half * NH:(half + 1) * NH], dt,
                                          ALU.add).then_inc(s_gate, 1)
                        dve.tensor_copy(gb[rows], ab[rows, :, (2 + half) * NH:(3 + half) * NH]).then_inc(s_gate, 1)
                    dve.wait_ge(s_gate, 4)
                    dve.tensor_scalar(gabs, ga, -1.0, None, ALU.mult).then_inc(s_gate, 1)
                    dve.wait_ge(s_gate, 5)
                    dve.tensor_tensor(gabs, gabs, ga, ALU.max).then_inc(s_gate, 1)
                    dve.wait_ge(s_gate, 6)
                    dve.tensor_scalar(ga, ga, 0.0, None, ALU.max).then_inc(s_gate, 1)
            high_part(16)
            for a in ada_before(3):
                ada_sum(a)
            for f in range(17, 20):
                high_part(f)
            dve.wait_ge(s_gact, 4)
            dve.tensor_tensor(ga, ga, gabs, ALU.add).then_inc(s_gate, 1)
            dve.tensor_scalar(gb, gb, 1.0, None, ALU.add).then_inc(s_gate, 1)
            dve.wait_ge(s_gate, 9)
            dve.scalar_tensor_tensor(k.g, ga, -1.0, expa.unsqueeze(1).to_broadcast([P, STEPS, NH]),
                                     ALU.mult, ALU.mult).then_inc(s_gate, 1)
            dve.reciprocal(k.beta, gb).then_inc(s_gate, 1)
            high_part(20)
            for a in ada_before(4):
                ada_sum(a)
            high_part(21)
            high_part(22)
            for f in range(NDN + 2 * FC, NT):
                if f + 3 < NT:
                    high_part(f + 3)
                if f % FC == 2:
                    for a in ada_before(f // FC):
                        ada_sum(a)
                if f == NT - FC:
                    dve.wait_ge(s_acol, 12)
                dve.wait_ge(k.s_tile, f + 1)
                dve.tensor_copy(na[:, f - NDN - FC, :].rearrange("p (b r c) -> p r b c", r=ROWS, c=KB),
                                psP[f % RING][:, :].rearrange("p (r b c) -> p r b c", r=ROWS, c=KB)
                                ).then_inc(s_evacv, 1)
                g = f - NDN - 2 * FC
                dve.wait_ge(s_ss, g + 1)
                if g:
                    dve.wait_ge(k.s_norm, g)
                dve.tensor_scalar(inv, psS[:, :], EPS, None, ALU.add).then_inc(s_inv, 1)
                dve.wait_ge(s_inv, 2 * g + 1)
                dve.reciprocal(inv, inv).then_inc(s_inv, 1)
                dve.wait_ge(s_root, g + 1)
                dve.scalar_tensor_tensor(qkv[:, g, :], inv, HD ** -0.5 if g < FC else 1.0, qkv[:, g, :],
                                         ALU.mult, ALU.mult).then_inc(k.s_norm, 1)


FLT_MAX = 3.4e38
WINDOW = [(0, 0), (1, 1), (3, 1), (4, 2)]
PAIRS = sorted({w + 2 * m for w, _ in WINDOW for m in range(2)})
DELTA = [0, -WIN // 2, -WIN]
A_KZ = 0
A_BIAS = M_HT
A_V = 2 * SLOT
A_MASKED = 4 * SLOT
A_P = SLOT
A_PT = SLOT + 4 * 512


def attend(k):
    nc = k.nc
    naq, nak, nav = (k.view(M_NA + i * FC * T, FC, T) for i in range(3))
    mix = k.view(M_MIX, 2 * FC, T)
    kz = k.view(A_KZ, FC, 2, T)
    bias = k.view(A_BIAS, NH, ROWS, QB)
    vw = k.view(A_V, len(PAIRS), HW)
    masked = k.view(A_MASKED, 3, NH, ROWS * WC)
    prob = [k.view(A_P + i * 512, 2, ROWS * WC) for i in range(4)]
    probT = [k.view(A_PT + i * 512, 2, 2, P) for i in range(4)]
    ident, window = k.const("ident"), k.const("window")
    largest, negmax, total, inverse = (k.misc(4, 2) for _ in range(4))

    s_kz = k.sem("s_kz")
    s_kzero = k.sem("s_kzero")
    s_masked = k.sem("s_masked")
    s_vt = k.sem("s_vt")
    s_vw = k.sem("s_vw")
    s_score = k.sem("s_score")
    s_biased = k.sem("s_biased")
    s_max = k.sem("s_max")
    s_exp = k.sem("s_exp")
    s_recip = k.sem("s_recip")
    s_prob = k.sem("s_prob")
    s_pt = k.sem("s_pt")
    s_ptout = k.sem("s_ptout")
    s_head = k.sem("s_head")
    s_headout = k.sem("s_headout")

    units = [(i, cc) for i in range(len(WINDOW)) for cc in range(FC)]
    N = len(units)
    psS = k.banks[0:3]
    psT = k.banks[3:5]
    psO = k.banks[5:7]

    with nc.Block() as block:
        @block.gpsimd
        def _(pool):
            pool.wait_ge(k.s_bias, 16)
            for d, delta in enumerate(DELTA):
                at = WIN + delta
                for b in range(WC // KB):
                    m = window[:, d * WC + b * KB:d * WC + (b + 1) * KB].unsqueeze(1).unsqueeze(1)
                    block_of = masked[:, d, :, b * ROWS * KB:(b + 1) * ROWS * KB].rearrange("p h (r c) -> p h r c", c=KB)
                    pool.tensor_tensor(block_of, bias[:, :, :, at + b * KB:at + (b + 1) * KB],
                                       m.to_broadcast([P, NH, ROWS, KB]), ALU.add).then_inc(s_masked, 1)

        @block.tensor
        def _(pe):
            for j, b in enumerate(PAIRS):
                if j >= 2:
                    pe.wait_ge(s_vw, j - 1)
                for cc in range(FC):
                    mm = pe.transpose(psT[j % 2][:, cc * P:(cc + 1) * P],
                                      nav[:, cc, b * ROWS * KB:b * ROWS * KB + P], ident)
                mm.then_inc(s_vt, 1)
            for u in range(N + 3):
                if u < N:
                    i, cc = units[u]
                    if i == 0:
                        pe.wait_ge(s_kz, 2 * (cc + 1))
                        pe.wait_ge(s_kzero, 2)
                    if u >= 3:
                        pe.wait_ge(s_biased, 2 * (u - 2))
                    at = WINDOW[i][0] * ROWS * KB
                    pe.matmul(psS[u % 3][:, :], naq[:, cc, i * P:(i + 1) * P], kz[:, cc, :, at:at + ROWS * WC],
                              start=True, stop=True).then_inc(s_score, 1)
                v = u - 2
                if 0 <= v < N:
                    pe.wait_ge(s_prob, 2 * v + 2)
                    if v < 2:
                        pe.wait_ge(s_vw, len(PAIRS))
                    else:
                        pe.wait_ge(s_ptout, v - 1)
                    for hp in range(2):
                        for m in range(2):
                            mm = pe.transpose(psT[v % 2][:, (2 * hp + m) * P:(2 * hp + m + 1) * P],
                                              prob[v % 4][:, hp, m * P:(m + 1) * P], ident)
                    mm.then_inc(s_pt, 1)
                v = u - 3
                if v >= 0:
                    i, cc = units[v]
                    pe.wait_ge(s_ptout, v + 1)
                    if v >= 2:
                        pe.wait_ge(s_headout, v - 1)
                    for m in range(2):
                        for hp in range(2):
                            h = 2 * cc + hp
                            mm = pe.matmul(psO[v % 2][hp * HD:(hp + 1) * HD, 0:P],
                                           vw[:, PAIRS.index(WINDOW[i][0] + 2 * m), h * HD:(h + 1) * HD], probT[v % 4][:, hp, m, :],
                                           start=(m == 0), stop=(m == 1))
                    mm.then_inc(s_head, 1)

        @block.vector
        def _(dve):
            for hp in range(2):
                dve.memset(kz[(1 - hp) * HD:(2 - hp) * HD, :, hp, :], 0.0).then_inc(s_kzero, 1)
            for cc in range(FC):
                for hp in range(2):
                    own = slice(hp * HD, (hp + 1) * HD)
                    dve.tensor_copy(kz[own, cc, hp, :], nak[own, cc, :]).then_inc(s_kz, 1)
            for u in range(N + 1):
                if u < N:
                    i, cc = units[u]
                    d = WINDOW[i][1]
                    dve.wait_ge(s_score, u + 1)
                    dve.wait_ge(s_masked, (d + 1) * (WC // KB))
                    if u >= 4:
                        dve.wait_ge(s_pt, u - 3)
                    for hp in range(2):
                        dve.tensor_tensor_reduce(
                            prob[u % 4][:, hp, :], psS[u % 3][:, hp * ROWS * WC:(hp + 1) * ROWS * WC],
                            masked[:, d, 2 * cc + hp, :], 1.0, -FLT_MAX, ALU.add, ALU.max,
                            accum_out=largest[:, u % 4, hp:hp + 1]).then_inc(s_biased, 1)
                    dve.wait_ge(s_biased, 2 * u + 2)
                    dve.tensor_scalar(negmax[:, u % 4, :], largest[:, u % 4, :], -1.0, None, ALU.mult).then_inc(s_max, 1)
                if u >= 1:
                    v = u - 1
                    dve.wait_ge(s_exp, 2 * v + 2)
                    dve.reciprocal(inverse[:, v % 4, :], total[:, v % 4, :]).then_inc(s_recip, 1)
                    dve.wait_ge(s_recip, v + 1)
                    for hp in range(2):
                        dve.tensor_scalar(prob[v % 4][:, hp, :], prob[v % 4][:, hp, :], inverse[:, v % 4, hp:hp + 1],
                                          None, ALU.mult).then_inc(s_prob, 1)

        @block.scalar
        def _(act):
            for j in range(len(PAIRS)):
                act.wait_ge(s_vt, j + 1)
                act.activation(vw[:, j, :], psT[j % 2][:, :], ACT.Copy).then_inc(s_vw, 1)
            for u in range(N + 3):
                if u < N:
                    act.wait_ge(s_max, u + 1)
                    for hp in range(2):
                        act.activation(prob[u % 4][:, hp, :], prob[u % 4][:, hp, :], ACT.Exp,
                                       bias=negmax[:, u % 4, hp:hp + 1],
                                       accum_out=total[:, u % 4, hp:hp + 1]).then_inc(s_exp, 1)
                v = u - 2
                if 0 <= v < N:
                    act.wait_ge(s_pt, v + 1)
                    if v >= 4:
                        act.wait_ge(s_head, v - 3)
                    act.activation(probT[v % 4].rearrange("p h m q -> p (h m q)"), psT[v % 2][:, :],
                                   ACT.Copy).then_inc(s_ptout, 1)
                v = u - 3
                if v >= 0:
                    i, cc = units[v]
                    act.wait_ge(s_head, v + 1)
                    act.activation(mix[:, FC + cc, :].rearrange("p (r c) -> p r c", c=GRID_W)[
                                       :, :, i * WIN:(i + 1) * WIN],
                                   psO[v % 2][:, 0:P].rearrange("p (r c) -> p r c", c=WIN),
                                   ACT.Copy).then_inc(s_headout, 1)


BLK = NH * P
D_TOKENS = 0
D_HEADS = D_TOKENS + 3 * FC * P
D_MA = D_HEADS + FC * 2 * 2 * P
D_U, D_T, D_X, D_KG, D_KT, D_QT = (D_MA + (2 + i) * BLK for i in range(6))
D_V, D_NEW, D_NEWT = (D_QT + BLK + i * HW for i in range(3))
D_SET = D_QT + BLK + 3 * HW
D_ODD = SPLIT - D_HEADS
D_STATE = [D_SET, D_ODD + D_SET]
D_DECAY = D_SET + HW
assert D_DECAY + 2 * HW <= D_ODD and D_STATE[1] + HW <= M_QKV
D_MASKED = M_NA + 2 * FC * T
HALVES = (slice(0, CH), slice(CH, P))
JOINS = LEVELS - 1
START = 1
PHASES = [("T", -1)] + [(what, j) for j in range(JOINS) for what in ("X", "U", "T")][:-1]
INV = len(PHASES)
SKEW = 2


def delta(k):
    nc = k.nc
    qkv = k.view(M_QKV, 3 * FC, T)
    mix = k.view(M_MIX, 2 * FC, T)
    zT = k.view(M_Z, FC, T)
    ident, uptoc, fold, levels = (k.const(n) for n in ("ident", "uptoc", "fold", "levels"))
    egc, etail, elast = k.misc(STEPS * NH), k.misc(STEPS * NH), k.misc(STEPS * NH)
    g_flat = k.g.rearrange("p s h -> p (s h)")
    beta_flat = k.beta.rearrange("p s h -> p (s h)")

    class Stream:
        def __init__(self, s):
            def buf(at, *shape):
                return k.view(s * D_ODD + at, *shape)
            self.tokens = buf(D_TOKENS, 3 * FC, 2, CH)
            self.heads = buf(D_HEADS, FC, 2, 2, P)
            self.ma = buf(D_MA, NH, 2, P)
            self.u, self.t, self.x, self.kg, self.kt, self.qt = (
                buf(at, NH, P) for at in (D_U, D_T, D_X, D_KG, D_KT, D_QT))
            self.w, self.qg = self.t, self.x
            self.v, self.new = buf(D_V, NH, HD), buf(D_NEW, NH, HD)
            self.newT = buf(D_NEWT, FC, P)
            self.g = k.view(D_MASKED + 2 * s * HW, NH, CH)
            self.beta = k.view(D_MASKED + (2 * s + 1) * HW, NH, CH)
            self.e = k.view(D_DECAY + s * HW, NH, CH)
            self.banks = k.banks[4 * s:4 * s + 4]
            self.old = k.view(D_STATE[s], NH, HD)
            self.next = k.view(D_STATE[1 - s], NH, HD)
            names = ("staged", "decay", "score", "exp", "em", "ma", "tok", "v", "kg", "qg", "u0", "w", "wout",
                     "q", "qout", "new", "newTout", "newp", "newout", "o", "oout", "ds", "dsout", "dst",
                     "scaled", "state")
            self.s = {n: k.sem(f"s_{n}{s}") for n in names}
            self.inv = [k.sem(f"s_inv{s}{h}") for h in range(2)]
            self.copied = [k.sem(f"s_copied{s}{h}") for h in range(2)]
            self.joined = [k.sem(f"s_joined{s}{h}") for h in range(2)]

    streams = [Stream(0), Stream(1)]
    other = {0: streams[1], 1: streams[0]}
    s_zero = k.sem("s_zero")
    s_zerop = k.sem("s_zerop")
    s_zeroa = k.sem("s_zeroa")
    s_gain = k.sem("s_gain")
    s_sums = k.sem("s_sums")
    s_esums = k.sem("s_esums")
    s_tailb = k.sem("s_tailb")
    s_turn = k.sem("s_turn")
    s_turnp = k.sem("s_turnp")
    s_turna = k.sem("s_turna")
    ITS = STEPS // 2

    def flat(ap):
        return ap.rearrange("p a b -> p (a b)")

    def heads4(bank):
        return bank[:, :].rearrange("p (h j) -> p h j", j=P)

    with nc.Block() as block:
        @block.sync
        def _(sp):
            sp.dma_start(k.view(W_OUT_NA, FC, D), k.dram["w_out"][HW:2 * HW].rearrange("(c p) n -> p c n", p=P)
                         ).then_inc(k.s_w_out[1], 16)
            sp.dma_start(k.view(M_WAB, KC, NG + NE), k.dram["w_route"].rearrange("(c p) n -> p c n", p=P)
                         ).then_inc(k.s_w_route, 16)

        @block.gpsimd
        def _(pool):
            def of_step(values, s, it):
                return values[:, bass.ds(it * (2 * NH) + s * NH, NH)].unsqueeze(2).to_broadcast([P, NH, CH])

            cols = uptoc.unsqueeze(1).to_broadcast([P, NH, CH])

            def stage_decays(s, it):
                st = streams[s]
                pool.wait_ge(st.s["decay"], it + START)
                pool.wait_ge(st.s["score"], it * FC + START)
                pool.wait_ge(st.s["tok"], it * 3 + START)
                pool.tensor_tensor(st.g, of_step(g_flat, s, it), cols, ALU.mult).then_inc(st.s["staged"], 1)

            def stage_betas(s, it):
                st = streams[s]
                pool.wait_ge(st.s["staged"], it * 8 + 7)
                pool.wait_ge(st.s["em"], it + START)
                pool.tensor_tensor(st.beta, of_step(beta_flat, s, it), cols, ALU.mult).then_inc(st.s["staged"], 1)

            def stage_tokens(s, it):
                st = streams[s]
                start = it * (2 * CH) + s * CH
                for d, at in enumerate((start, (STEPS - 1) * CH - start)):
                    pool.tensor_copy(st.tokens[:, :, d, :], qkv[:, :, bass.ds(at, CH)]).then_inc(st.s["staged"], 1)
                pool.wait_ge(s_zerop, s + 1)
                pool.wait_ge(st.s["staged"], it * 8 + 3)
                pool.sem_inc(s_turnp, 1)
                for hp in range(2):
                    own = HALVES[hp]
                    if hp:
                        pool.wait_ge(st.s["staged"], it * 8 + 5)
                        pool.sem_inc(s_turnp, 1)
                    for qk in range(2):
                        pool.tensor_copy(
                            st.heads[own, :, hp, qk, :],
                            st.tokens[own, qk * FC:(qk + 1) * FC].rearrange("p a b c -> p a (b c)")
                            ).then_inc(st.s["staged"], 1)

            for stage in (stage_decays, stage_betas):
                for s in range(2):
                    stage(s, 0)
            with pool.Fori(1, ITS) as it:
                for s in range(2):
                    stage_decays(s, it)
                    stage_tokens(s, it)
                    stage_betas(s, it)

            for cc in range(FC):
                pool.tensor_scalar(zT[:, cc, :], zT[:, cc, :], k.col(C_ONORM), None, ALU.mult).then_inc(s_gain, 1)

        @block.tensor
        def _(pe):
            for st in streams:
                for name in ("decay", "score", "tok", "new", "o"):
                    pe.sem_inc(st.s[name], START)
            for i, name in enumerate(("upto", "after", "halves")):
                pe.matmul(k.banks[i][:, 0:STEPS * NH], k.const(name), g_flat, start=True, stop=True).then_inc(s_sums, 1)
            pe.wait_ge(s_esums, 3)

            def decays(st, it):
                pe.wait_ge(st.s["staged"], it * 8 + 1)
                pe.wait_ge(st.s["oout"], it * 2 + START)
                pe.matmul(st.banks[0][:, :], k.const("after"), flat(st.g), start=True,
                          stop=True).then_inc(st.s["decay"], 1)

            def scores(st, it, cc):
                s = st.s
                if cc == 0:
                    pe.wait_ge(s["staged"], it * 8 + 7)
                    pe.wait_ge(s["dsout"], it + START)
                elif cc == 1:
                    pe.wait_ge(s["state"], it + START)
                elif cc == 2:
                    pe.wait_ge(s["newout"], it + START)
                else:
                    pe.wait_ge(s["exp"], it + 1)
                for d, rows in enumerate(HALVES):
                    mm = pe.matmul(st.banks[(cc + 1) % 4][rows, 0:4 * CH], st.tokens[:, FC + cc, d, :],
                                   st.heads[:, cc, :, :, rows], start=True, stop=True)
                mm.then_inc(s["score"], 1)

            def on_partitions(st, it, i):
                pe.wait_ge(st.s["ma"], it * 8 + 2 * (i + 1) + START)
                for cc in range(FC):
                    mm = pe.transpose(st.banks[i + 1][:, cc * P:(cc + 1) * P],
                                      st.tokens[:, (2, 1, 0)[i] * FC + cc].rearrange("p a b -> p (a b)"), ident)
                mm.then_inc(st.s["tok"], 1)

            def prepare(st, it):
                decays(st, it)
                for cc in range(FC):
                    scores(st, it, cc)
                for i in range(3):
                    on_partitions(st, it, i)

            def invert(st, it, n):
                what, j = PHASES[n]
                for half in range(2):
                    bank = heads4(st.banks[half])
                    if what == "T":
                        pe.wait_ge(st.joined[half], it * LEVELS + j + 2)
                        if j < 0 and half == 0:
                            pe.wait_ge(st.s["ma"], it * 8 + 8 + START)
                        if j < 0 and half == 1:
                            pe.wait_ge(st.s["v"], it + 1)
                    elif what == "X":
                        pe.wait_ge(st.copied[half], it * (2 * JOINS) + 2 * j + 1)
                    else:
                        pe.wait_ge(st.copied[half], it * (2 * JOINS) + 2 * j + 2)
                    for i in range(NH // 2):
                        h = half * (NH // 2) + i
                        if what == "T":
                            mm = pe.transpose(bank[:, i, :], st.u[:, h, :], ident)
                        elif what == "X":
                            mm = pe.matmul(bank[:, i, :], st.ma[:, h, 1, :], st.t[:, h, :], start=True, stop=True)
                        else:
                            mm = pe.matmul(bank[:, i, :], st.x[:, h, :], st.u[:, h, :], start=True, stop=True)
                    mm.then_inc(st.inv[half], 1)

            def weights(st, it, half):
                pe.wait_ge(st.joined[half], it * LEVELS + LEVELS)
                if half == 0:
                    pe.wait_ge(st.s["kg"], it * 4 + 4)
                else:
                    pe.wait_ge(st.s["qg"], it * 2 + 2)
                for i in range(NH // 2):
                    h = half * (NH // 2) + i
                    mm = pe.matmul(heads4(st.banks[2 + half])[:, i, :], st.kg[:, h, :], st.u[:, h, :],
                                   start=True, stop=True)
                mm.then_inc(st.s["w"], 1)

            def queries(st, half):
                for i in range(NH // 2):
                    h = half * (NH // 2) + i
                    mm = pe.transpose(heads4(st.banks[half])[:, i, :], st.qg[:, h, :], ident)
                mm.then_inc(st.s["q"], 1)

            def new_values(n, it):
                st = streams[n]
                pe.wait_ge(st.s["wout"], it * 2 + 2)
                pe.wait_ge(other[n].s["state"], it + n + START)
                for cc in range(FC):
                    for i in range(2):
                        for hp in range(2):
                            h = 2 * cc + hp
                            left, right = ((st.v, st.u), (st.old, st.w))[i]
                            mm = pe.matmul(st.banks[2][hp * HD:(hp + 1) * HD, cc * P:(cc + 1) * P], left[:, h, :],
                                           right[:, h, :], start=(i == 0), stop=(i == 1))
                mm.then_inc(st.s["new"], 1)

            def new_on_partitions(st, it):
                pe.wait_ge(st.s["newTout"], it + 1)
                for cc in range(FC):
                    mm = pe.transpose(st.banks[3][:, cc * P:(cc + 1) * P], st.newT[:, cc, :], ident)
                mm.then_inc(st.s["newp"], 1)

            def increment(st, it):
                pe.wait_ge(st.s["newout"], it + 1 + START)
                pe.wait_ge(st.s["qout"], it * 2 + 2)
                for cc in range(FC):
                    for hp in range(2):
                        h = 2 * cc + hp
                        mm = pe.matmul(st.banks[1][hp * HD:(hp + 1) * HD, cc * P:(cc + 1) * P], st.new[:, h, :],
                                       st.kt[:, h, :], start=True, stop=True)
                mm.then_inc(st.s["ds"], 1)

            def outputs(st):
                for cc in range(FC):
                    for i in range(2):
                        for hp in range(2):
                            h = 2 * cc + hp
                            left, right = ((st.old, st.qt[:, h, :]), (st.new, st.ma[:, h, 0, :]))[i]
                            mm = pe.matmul(st.banks[0][hp * HD:(hp + 1) * HD, cc * P:(cc + 1) * P], left[:, h, :],
                                           right, start=(i == 0), stop=(i == 1))
                mm.then_inc(st.s["o"], 1)

            def increment_back(st, it):
                pe.wait_ge(st.s["dsout"], it + 1 + START)
                for cc in range(FC):
                    mm = pe.transpose(st.banks[2][:, cc * P:(cc + 1) * P], st.newT[:, cc, :], ident)
                mm.then_inc(st.s["dst"], 1)

            def steps(it, last):
                even, odd = streams
                for n in range(INV + SKEW):
                    if n < INV:
                        invert(even, it, n)
                    if n == 0:
                        decays(odd, it)
                        for cc in range(FC):
                            scores(odd, it, cc)
                    if n == 1:
                        for i in range(3):
                            on_partitions(odd, it, i)
                    if n >= SKEW:
                        invert(odd, it, n - SKEW)
                    if n >= INV:
                        weights(even, it, n - INV)
                queries(even, 0)
                new_values(0, it)
                queries(even, 1)
                weights(odd, it, 0)
                new_on_partitions(even, it)
                weights(odd, it, 1)
                queries(odd, 0)
                increment(even, it)
                outputs(even)
                increment_back(even, it)
                queries(odd, 1)
                new_values(1, it)
                if not last:
                    decays(even, it + 1)
                    scores(even, it + 1, 0)
                new_on_partitions(odd, it)
                if not last:
                    scores(even, it + 1, 1)
                    scores(even, it + 1, 2)
                increment(odd, it)
                if not last:
                    scores(even, it + 1, 3)
                outputs(odd)
                if not last:
                    on_partitions(even, it + 1, 0)
                increment_back(odd, it)
                if not last:
                    on_partitions(even, it + 1, 1)
                    on_partitions(even, it + 1, 2)

            prepare(streams[0], 0)
            with pe.Fori(0, ITS - 1) as it:
                steps(it, last=False)
            steps(ITS - 1, last=True)

        @block.scalar
        def _(act):
            for st in streams:
                for name in ("dsout", "newout"):
                    act.sem_inc(st.s[name], START)
            act.wait_ge(s_sums, 3)
            for i, e in enumerate((egc, etail, elast)):
                act.activation(e, k.banks[i][:, 0:STEPS * NH], ACT.Exp).then_inc(s_esums, 1)
            def stage_first(s):
                st = streams[s]
                act.wait_ge(st.s["staged"], 1)
                for d, at in enumerate((s * CH, (STEPS - 1 - s) * CH)):
                    act.activation(st.tokens[:, :, d, :], qkv[:, :, at:at + CH], ACT.Copy).then_inc(st.s["staged"], 1)
                act.wait_ge(s_zerop, s + 1)
                act.wait_ge(st.s["staged"], 3)
                act.sem_inc(s_turna, 1)
                for hp in range(2):
                    own = HALVES[hp]
                    for qk in range(2):
                        act.activation(st.heads[own, :, hp, qk, :],
                                       st.tokens[own, qk * FC:(qk + 1) * FC].rearrange("p a b c -> p a (b c)"),
                                       ACT.Copy).then_inc(st.s["staged"], 1)

            def decays(st, it):
                act.wait_ge(st.s["decay"], it + 1 + START)
                act.wait_ge(st.s["ma"], it * 8 + START)
                act.activation(flat(st.e), st.banks[0][:, :], ACT.Exp).then_inc(st.s["exp"], 1)

            stage_first(0)
            decays(streams[0], 0)
            stage_first(1)
            zeros = [k.between(M_C, M_C + 1024), k.between(M_C, M_C + HW)]
            for b in (streams[0].kg, streams[0].kt, streams[1].kg, streams[1].kt, mix[:, 0:2, :], mix[:, 2:4, :]):
                act.activation(flat(b), zeros[0], ACT.Copy, scale=0.0).then_inc(s_zeroa, 1)
            act.activation(flat(streams[0].old), zeros[1], ACT.Copy, scale=0.0).then_inc(s_zeroa, 1)

            def values(st, it):
                act.wait_ge(st.s["tok"], it * 3 + 1 + START)
                act.wait_ge(st.s["new"], it + START)
                act.activation(flat(st.v), st.banks[1][:, :], ACT.Copy).then_inc(st.s["v"], 1)

            def invert(st, it, n):
                what, j = PHASES[n]
                for half in range(2):
                    hs = slice(half * NH // 2, (half + 1) * NH // 2)
                    if what == "X":
                        act.wait_ge(st.inv[half], INV * it + n + 1)
                        act.activation(flat(st.x[:, hs]), st.banks[half][:, :], ACT.Copy,
                                       scale=-1.0).then_inc(st.copied[half], 1)
                    elif what == "T":
                        act.wait_ge(st.inv[half], INV * it + n + 1)
                        act.activation(flat(st.t[:, hs]), st.banks[half][:, :], ACT.Copy).then_inc(st.copied[half], 1)

            def weights(st, it, half):
                hs = slice(half * NH // 2, (half + 1) * NH // 2)
                act.wait_ge(st.s["w"], it * 2 + half + 1)
                act.activation(flat(st.w[:, hs]), st.banks[2 + half][:, :], ACT.Copy,
                               scale=-1.0).then_inc(st.s["wout"], 1)

            def queries(st, it, half):
                hs = slice(half * NH // 2, (half + 1) * NH // 2)
                act.wait_ge(st.s["q"], it * 2 + half + 1)
                act.activation(flat(st.qt[:, hs]), st.banks[half][:, :], ACT.Copy).then_inc(st.s["qout"], 1)

            def new_values(st, it):
                act.wait_ge(st.s["new"], it + 1 + START)
                act.activation(flat(st.newT), st.banks[2][:, :], ACT.Copy).then_inc(st.s["newTout"], 1)

            def new_on_partitions(st, it):
                act.wait_ge(st.s["newp"], it + 1)
                act.activation(flat(st.new), st.banks[3][:, :], ACT.Copy).then_inc(st.s["newout"], 1)

            def increment(st, it):
                act.wait_ge(st.s["ds"], it + 1)
                act.activation(flat(st.newT), st.banks[1][:, :], ACT.Copy).then_inc(st.s["dsout"], 1)

            def steps(it, last):
                even, odd = streams
                values(even, it)
                for n in range(INV + SKEW):
                    if n < INV:
                        invert(even, it, n)
                    if n == 0:
                        decays(odd, it)
                    if n == 1:
                        values(odd, it)
                    if n >= SKEW:
                        invert(odd, it, n - SKEW)
                    if n >= INV:
                        weights(even, it, n - INV)
                queries(even, it, 0)
                new_values(even, it)
                queries(even, it, 1)
                weights(odd, it, 0)
                new_on_partitions(even, it)
                weights(odd, it, 1)
                queries(odd, it, 0)
                increment(even, it)
                queries(odd, it, 1)
                new_values(odd, it)
                if not last:
                    decays(even, it + 1)
                new_on_partitions(odd, it)
                increment(odd, it)

            with act.Fori(0, ITS - 1) as it:
                steps(it, last=False)
            steps(ITS - 1, last=True)

        @block.vector
        def _(dve):
            for st in streams:
                for name in ("em", "oout", "state", "ma"):
                    dve.sem_inc(st.s[name], START)
            def zero_blocks(st):
                dve.memset(st.ma.rearrange("p a b c -> p (a b c)"), 0.0).then_inc(s_zero, 1)
                dve.memset(flat(st.u), 0.0).then_inc(s_zero, 1)

            for st in streams:
                dve.memset(st.heads.rearrange("p a b c d -> p (a b c d)"), 0.0).then_inc(s_zerop, 1)
            zero_blocks(streams[0])
            dve.wait_ge(s_zero, 2)
            dve.wait_ge(s_esums, 3)
            dve.tensor_tensor(etail, etail, beta_flat, ALU.mult).then_inc(s_tailb, 1)
            dve.wait_ge(s_tailb, 1)

            def scores(n, it):
                st = streams[n]
                s, b = st.s, st.banks
                dve.wait_ge(s["exp"], it + 1)
                dve.wait_ge(s["staged"], it * 8 + 8)
                dve.tensor_tensor(st.e, st.e, st.beta, ALU.mult).then_inc(s["em"], 1)
                dve.wait_ge(s["em"], it + 1 + START)
                for cc in range(FC):
                    dve.wait_ge(s["score"], it * FC + cc + 1 + START)
                    both = b[(cc + 1) % 4][:, 0:4 * CH].rearrange("p (h m j) -> p h m j", h=2, m=2)
                    for d, rows in enumerate(HALVES):
                        c = slice(d * CH, (d + 1) * CH)
                        e = st.e[rows, 2 * cc:2 * cc + 2].unsqueeze(2).to_broadcast([CH, 2, 2, CH])
                        dve.tensor_tensor(st.ma[rows, 2 * cc:2 * cc + 2, :, c], both[rows], e,
                                          ALU.mult).then_inc(s["ma"], 1)

            def first_join(n, it):
                st = streams[n]
                s = st.s
                dve.wait_ge(s["ma"], it * 8 + 8 + START)
                for half in range(2):
                    hs = slice(half * NH // 2, (half + 1) * NH // 2)
                    for d, rows in enumerate(HALVES):
                        c = slice(d * CH, (d + 1) * CH)
                        mask = levels[rows, 0:CH].unsqueeze(1).to_broadcast([CH, NH // 2, CH])
                        dve.scalar_tensor_tensor(st.u[rows, hs, c], st.ma[rows, hs, 1, c], -1.0, mask,
                                                 ALU.mult, ALU.mult).then_inc(s["u0"], 1)
                    dve.wait_ge(s["u0"], it * 4 + 2 * half + 2)
                    dve.tensor_tensor(st.u[:, hs], st.u[:, hs], ident.unsqueeze(1).to_broadcast([P, NH // 2, P]),
                                      ALU.add).then_inc(st.joined[half], 1)

            def keys(n, it):
                st = streams[n]
                dve.wait_ge(st.s["tok"], it * 3 + 2 + START)
                tok = st.banks[2][:, :].rearrange("p (h j) -> p h j", j=HD)
                for d, rows in enumerate(HALVES):
                    c = slice(d * CH, (d + 1) * CH)
                    for dst, e in ((st.kg, egc), (st.kt, etail)):
                        e = e[rows, bass.ds(it * (2 * NH) + n * NH, NH)].unsqueeze(2).to_broadcast([CH, NH, HD])
                        dve.tensor_tensor(dst[rows, :, c], tok[rows], e, ALU.mult).then_inc(st.s["kg"], 1)

            def join(n, it, j):
                st = streams[n]
                for half in range(2):
                    hs = slice(half * NH // 2, (half + 1) * NH // 2)
                    bank = heads4(st.banks[half])
                    dve.wait_ge(st.inv[half], it * INV + 3 * j + 3)
                    dve.wait_ge(st.joined[half], it * LEVELS + j + 1)
                    dve.sem_inc(s_turn, 1)
                    for d, rows in enumerate(HALVES):
                        c = slice(d * CH, (d + 1) * CH)
                        mask = levels[rows, (j + 1) * CH:(j + 2) * CH].bitcast(U32)
                        ins = dve.copy_predicated(st.u[rows, hs, c], mask.unsqueeze(1).to_broadcast([CH, NH // 2, CH]),
                                                  bank[rows, :, c])
                    ins.then_inc(st.joined[half], 1)

            def queries(n, it):
                st = streams[n]
                dve.wait_ge(st.s["tok"], it * 3 + 3 + START)
                tok = st.banks[3][:, :].rearrange("p (h j) -> p h j", j=HD)
                for d, rows in enumerate(HALVES):
                    c = slice(d * CH, (d + 1) * CH)
                    e = egc[rows, bass.ds(it * (2 * NH) + n * NH, NH)].unsqueeze(2).to_broadcast([CH, NH, HD])
                    dve.tensor_tensor(st.qg[rows, :, c], tok[rows], e, ALU.mult).then_inc(st.s["qg"], 1)

            def outputs_and_state(n, it):
                st = streams[n]
                s, b = st.s, st.banks
                dve.wait_ge(other[n].s["state"], it + n + START)
                dve.wait_ge(other[n].s["o"], it + n + START)
                e = elast[:, bass.ds(it * (2 * NH) + n * NH, NH)].unsqueeze(2).to_broadcast([P, NH, HD])
                dve.tensor_tensor(st.next, st.old, e, ALU.mult).then_inc(s["scaled"], 1)
                dve.wait_ge(s["o"], it + 1 + START)
                dve.wait_ge(other[n].s["oout"], 2 * it + 2 * n + START)
                o = b[0][:, :].rearrange("p (a d c) -> p a d c", d=2, c=CH)
                start = it * (2 * CH) + n * CH
                for d, at in enumerate((start, (STEPS - 1) * CH - start)):
                    at = mix[:, 0:FC, bass.ds(at, CH)]
                    dve.tensor_tensor(at, at, o[:, :, d, :], ALU.add).then_inc(s["oout"], 1)
                dve.wait_ge(s["dst"], it + 1)
                dve.wait_ge(s["scaled"], it + 1)
                dve.tensor_tensor(flat(st.next), flat(st.next), b[2][:, :], ALU.add).then_inc(s["state"], 1)

            def steps(it, last):
                scores(1, it)
                first_join(1, it)
                for j in range(JOINS):
                    join(0, it, j)
                    if j == 0:
                        keys(0, it)
                    if j == JOINS - 1:
                        queries(0, it)
                    join(1, it, j)
                    if j == 0:
                        keys(1, it)
                queries(1, it)
                outputs_and_state(0, it)
                if not last:
                    scores(0, it + 1)
                outputs_and_state(1, it)
                if not last:
                    first_join(0, it + 1)

            scores(0, 0)
            first_join(0, 0)
            zero_blocks(streams[1])
            dve.wait_ge(s_zero, 4)
            dve.sem_inc(s_turn, 1)
            with dve.Fori(0, ITS - 1) as it:
                steps(it, last=False)
            steps(ITS - 1, last=True)


BUFFERS = 3
GATE_UP_AT = [0, 4 * SLOT, M_QKV + TT * D]
DOWN_AT = [2 * SLOT, 3 * SLOT, M_NA]


def load_expert(sp, k, e, place, static=True, parts=(0, 1, 2)):
    for i in parts:
        name, rows = (("w_gate", KC), ("w_up", KC), ("w_down", DE // P))[i]
        src = k.dram[name][e] if static else k.dram[name][bass.ds(e, 1)].rearrange("a r n -> (a r) n")
        at = (GATE_UP_AT[place], GATE_UP_AT[place] + SLOT, DOWN_AT[place])[i]
        sp.dma_start(k.view(at, rows, SLOT // rows),
                     src.rearrange("(c p) n -> p c n", p=P)).then_inc(k.s_expert[place][i], 16)


M_X1 = M_HT
M_GT1 = M_NA + TT * D
M_GT2 = M_GT1 + D
M_A2 = M_Z
M_B2 = M_Z + D
M_H2 = M_QKV
M_DIAG = M_QKV + TT * D
H2T_AT = 3 * SLOT
W_OUT_DN = 4 * SLOT
W_OUT_NA = M_NA
NORM_AT = 5 * SLOT
ITEMS_MAX = NE + 2 * T // SL
ROWS_OUT = 2 * T


def route(k):
    nc, dram = k.nc, k.dram
    mixT = k.view(M_MIX, KC, T)
    w_out = [k.view(W_OUT_DN, FC, D), k.view(W_OUT_NA, FC, D)]
    zT = k.view(M_Z, FC, T)
    squares = k.view(NORM_AT, FC, T)
    inv = k.view(NORM_AT + FC * T, TT, NH)
    invT = k.view(NORM_AT + FC * T + TT * NH, T)
    spread_head = k.view(NORM_AT + FC * T + TT * NH + T, HW)
    w_route = k.view(M_WAB, KC, NG + NE)
    x1 = k.view(M_X1, TT, D)
    h2 = k.view(M_H2, TT, D)
    h2T = k.view(H2T_AT, KC, T)
    rows = k.view(M_GT1, D), k.view(M_A2, D), k.view(M_B2, D), k.view(M_GT2, D)
    diag = [k.view(M_DIAG + i * P, P) for i in range(4)]
    junk = k.view(M_DIAG + 512, D)
    logitsT = k.view(M_DIAG + 1536, T)
    ident = k.const("ident")
    k.misc_at = k.free_misc
    k.weight = [k.misc(TT), k.misc(TT)]
    k.row = [k.misc(TT).bitcast(I32), k.misc(TT).bitcast(I32)]
    k.place = k.misc(TT, NE)
    items = k.misc(3, ITEMS_MAX + 1).bitcast(I32)
    k.item_e, k.item_place, k.item_row = (items[:, i, :] for i in range(3))
    k.tiles = k.misc(NE).bitcast(I32)
    k.upto = k.misc(NE).bitcast(I32)
    k.total = k.upto[:, NE - 1:NE]
    col = k.misc(3 * KC)
    ss, ss2, rs = k.misc(2, TT), k.misc(TT), k.misc(2, TT)
    logits = k.misc(TT, NG + NE)
    first = k.misc(EG)
    gmax, gexp, gsum, geq, gbest, gone = k.misc(TT), k.misc(TT, NG), k.misc(TT), k.misc(TT, NG), k.misc(TT), k.misc(TT, NG)
    per_group, ing = k.misc(TT, NG, EG), k.misc(TT, EG)
    top, eq, best = [k.misc(TT), k.misc(TT)], k.misc(TT, EG), k.misc(TT)
    one = [k.misc(TT, EG), k.misc(TT, EG)]
    chosen = [k.misc(TT, NE), k.misc(TT, NE)]
    ratio, denom = k.misc(TT), k.misc(TT)
    both, both_sum = k.misc(TT, NE), k.misc(NE)
    rank = k.misc(TT, NE)
    over = k.view(M_DIAG, NE, T // SL - 1)
    summed = k.misc(3, NE)
    tiles, count = summed[:, 1, :], summed[:, 2, :]
    cum, before = k.misc(2, NE), k.misc(NE)
    index, past, past_sums, item = k.misc(1), k.misc(NE), k.misc(3), k.misc(3)
    numbered, spare = k.misc(P), k.misc(3, NE)

    s_osq = k.sem("s_osq")
    s_oss = k.sem("s_oss")
    s_oinv = k.sem("s_oinv")
    s_oroot = k.sem("s_oroot")
    s_sel = k.sem("s_sel")
    s_oT = k.sem("s_oT")
    s_oTout = k.sem("s_oTout")
    s_ospread = k.sem("s_ospread")
    s_gated = k.sem("s_gated")
    s_normed = k.sem("s_normed")
    s_x1in = k.sem("s_x1in")
    s_col = k.sem("s_col")
    s_diag = k.sem("s_diag")
    s_row = k.sem("s_row")
    s_rowout = k.sem("s_rowout")
    s_y = k.sem("s_y")
    s_ysq = k.sem("s_ysq")
    s_yms = k.sem("s_yms")
    s_yroot = k.sem("s_yroot")
    s_yout = k.sem("s_yout")
    s_x1 = k.sem("s_x1")
    s_xsq = k.sem("s_xsq")
    s_h2 = k.sem("s_h2")
    s_h2T = k.sem("s_h2T")
    s_h2Tout = k.sem("s_h2Tout")
    s_logit = k.sem("s_logit")
    s_logitout = k.sem("s_logitout")
    s_logitp = k.sem("s_logitp")
    s_r = k.sem("s_r")
    s_rexp = k.sem("s_rexp")
    s_both = k.sem("s_both")
    s_rank = k.sem("s_rank")
    s_rankout = k.sem("s_rankout")
    s_place = k.sem("s_place")
    s_index = k.sem("s_index")
    s_item = k.sem("s_item")
    s_itemrow = k.sem("s_itemrow")
    s_xms = k.sem("s_xms")
    s_xroot = k.sem("s_xroot")
    s_gshift = k.sem("s_gshift")
    s_diff = k.sem("s_diff")

    ROWS_AT = [(0, 0), (1, 0), (2, 1), (2, 0)]
    psY = [k.banks[0:2], k.banks[2:4]]
    psT = k.banks[4:6]
    psR = k.banks[6]
    psL = k.banks[7]
    psO = [k.banks[i] for i in (4, 5, 7, 6)]
    psN, psNT = k.banks[7], k.banks[6]

    with nc.Block() as block:
        @block.sync
        def _(sp):
            sp.dma_start(w_out[0], dram["w_out"][0:HW].rearrange("(c p) n -> p c n", p=P)).then_inc(k.s_w_out[0], 16)
            sp.dma_start(x1, dram["x"].rearrange("(t p) d -> p t d", p=P)).then_inc(s_x1in, 16)
            load_expert(sp, k, 0, 0)
            sp.wait_ge(s_normed, FC)
            load_expert(sp, k, 1, 1, parts=(1,))
            sp.wait_ge(s_y, 2 * TT)
            load_expert(sp, k, 1, 1, parts=(0,))
            load_expert(sp, k, 2, 2, parts=(2,))
            sp.wait_ge(s_logit, 3)
            load_expert(sp, k, 1, 1, parts=(2,))

        @block.gpsimd
        def _(pool):
            for cc in range(FC):
                pool.wait_ge(s_osq, cc + 1)
                pool.tensor_tensor(mixT[:, cc, :], mixT[:, cc, :], zT[:, cc, :], ALU.mult).then_inc(s_gated, 1)
            pool.wait_ge(s_rankout, 1)
            for t in range(1, TT):
                pool.tensor_tensor(rank[:, t, :], rank[:, t - 1, :], both[:, t - 1, :], ALU.add).then_inc(s_place, 1)
                pool.wait_ge(s_place, t)
            pool.tensor_scalar(k.place, rank, 1.0, None, ALU.add).then_inc(s_place, 1)
            pool.wait_ge(s_place, TT)
            pool.tensor_tensor(k.place, k.place, both, ALU.mult).then_inc(s_place, 1)
            pool.wait_ge(s_place, TT + 1)
            pool.tensor_scalar(k.place, k.place, -1.0, None, ALU.add).then_inc(s_place, 1)

        @block.tensor
        def _(pe):
            def columns_to_rows(group):
                for n in range(4 * group, 4 * group + 4):
                    pe.wait_ge(s_diag, n + 1)
                    if n % 4 == 0 and n >= 4:
                        pe.wait_ge(s_rowout, n // 4)
                    pe.matmul(psR[:, (n % 4) * P:(n % 4 + 1) * P], k.const("ones"), diag[n % 4],
                              start=True, stop=True).then_inc(s_row, 1)

            def project_out(t, part, halves=(0, 1)):
                for i in halves:
                    for c in range(FC):
                        if t == 0 and i == 0 and part == 0:
                            pe.wait_ge(s_normed, c + 1)
                        mm = pe.matmul(psY[t % 2][i][:, :], mixT[:, part * FC + c, t * P:(t + 1) * P],
                                       w_out[part][:, c, i * 512:(i + 1) * 512],
                                       start=(part == 1 and c == 0), stop=(part == 0 and c == FC - 1))
                    if part == 0:
                        mm.then_inc(s_y, 1)
                    if (t, part) in ROWS_AT:
                        columns_to_rows(ROWS_AT.index((t, part)) * 2 + i)

            def logits_of(first, end):
                pe.wait_ge(k.s_w_route, 16)
                pe.wait_ge(s_h2Tout, 2 * end)
                for c in range(KC):
                    mm = pe.matmul(psL[0:NG + NE, first * P:end * P], w_route[:, c, :], h2T[:, c, first * P:end * P],
                                   start=(c == 0), stop=(c == KC - 1))
                mm.then_inc(s_logit, 1)

            pe.wait_ge(k.s_w_out[1], 16)
            project_out(0, 1, halves=(0,))
            pe.wait_ge(s_osq, FC)
            for t in range(TT):
                for cc in range(FC):
                    at = t * NH + 2 * cc
                    mm = pe.matmul(psN[:, at:at + 2], squares[:, cc, t * P:(t + 1) * P],
                                   k.const("halves")[:, 0:P:HD], start=True, stop=True)
            mm.then_inc(s_oss, 1)
            project_out(0, 1, halves=(1,))
            pe.wait_ge(s_oroot, 1)
            for t in range(TT):
                mm = pe.transpose(psNT[0:NH, t * P:(t + 1) * P], inv[:, t, :], ident)
            mm.then_inc(s_oT, 1)
            project_out(1, 1, halves=(0,))
            pe.wait_ge(s_oTout, 1)
            pe.wait_ge(s_sel, 1)
            for cc in range(FC):
                pe.matmul(psO[cc][:, :], spread_head[0:NH, cc * P:(cc + 1) * P], invT[0:NH, :], start=True, stop=True).then_inc(s_ospread, 1)
            project_out(1, 1, halves=(1,))
            pe.wait_ge(k.s_w_out[0], 16)
            for t in range(TT + 2):
                if t < TT:
                    if t >= 2:
                        pe.wait_ge(s_yout, 2 * (t - 2) + 2)
                        project_out(t, 1)
                    project_out(t, 0)
                if t >= 2:
                    v = t - 2
                    if v == 2:
                        logits_of(0, 2)
                    pe.wait_ge(s_h2, 2 * v + 2)
                    for c in range(KC):
                        if c % 4 == 0 and v:
                            pe.wait_ge(s_h2Tout, 2 * (v - 1) + c // 4 + 1)
                        mm = pe.transpose(psT[c // 4][:, (c % 4) * P:(c % 4 + 1) * P],
                                          h2[:, v, c * P:(c + 1) * P], ident)
                        if c % 4 == 3:
                            mm.then_inc(s_h2T, 1)
            logits_of(2, 3)
            logits_of(3, 4)
            pe.wait_ge(s_logitout, 1)
            pe.wait_ge(s_rowout, KC)
            for t in range(TT):
                mm = pe.transpose(psR[:, t * 64:t * 64 + NG + NE], logitsT[0:NG + NE, t * P:(t + 1) * P],
                                  ident[0:NG + NE, 0:NG + NE])
            mm.then_inc(s_logitp, 1)
            pe.wait_ge(s_both, 1)
            pe.matmul(psT[0][:, 0:NE], k.const("before"), both_sum, start=True, stop=True).then_inc(s_rank, 1)
            pe.matmul(psT[1][:, 0:NE], k.const("ones"), both_sum, start=True, stop=True).then_inc(s_rank, 1)
            pe.wait_ge(s_item, 3)
            for i in range(3):
                mm = pe.matmul(psL[0:1, i * 64:i * 64 + ITEMS_MAX + 1], item[0:ITEMS_MAX + 1, i:i + 1],
                               ident[0:ITEMS_MAX + 1, 0:ITEMS_MAX + 1], start=True, stop=True)
            mm.then_inc(s_itemrow, 1)

        @block.scalar
        def _(act):
            for cc in range(FC):
                act.activation(squares[:, cc, :], mixT[:, cc, :], ACT.Square).then_inc(s_osq, 1)
            act.wait_ge(s_oinv, 2)
            act.activation(inv, inv, ACT.Sqrt).then_inc(s_oroot, 1)
            act.wait_ge(s_oT, 1)
            act.activation(invT[0:NH, :], psNT[0:NH, :], ACT.Copy).then_inc(s_oTout, 1)
            def h2T_out(v):
                for i in range(2):
                    act.wait_ge(s_h2T, 2 * v + i + 1)
                    act.activation(h2T[:, 4 * i:4 * i + 4, v * P:(v + 1) * P],
                                   psT[i][:, :].rearrange("p (c j) -> p c j", j=P), ACT.Copy).then_inc(s_h2Tout, 1)

            for t in range(TT + 2):
                if t < TT:
                    for i in range(2):
                        act.wait_ge(s_y, 2 * t + i + 1)
                        if t or i:
                            act.wait_ge(s_ysq, 2 * t + i)
                        if t and i == 0:
                            act.wait_ge(s_xsq, t)
                        act.activation(junk[:, 0:512], psY[t % 2][i][:, :], ACT.Square,
                                       accum_out=ss[:, i, t:t + 1]).then_inc(s_ysq, 1)
                    act.wait_ge(s_yms, 3 * (t + 1))
                    act.activation(rs[:, 0, t:t + 1], rs[:, 0, t:t + 1], ACT.Sqrt).then_inc(s_yroot, 1)
                    if t >= 2:
                        h2T_out(t - 2)
                    act.wait_ge(s_x1, t + 1)
                    act.wait_ge(s_ysq, 2 * t + 2)
                    act.activation(junk, x1[:, t, :], ACT.Square, accum_out=ss2[:, t:t + 1]).then_inc(s_xsq, 1)
                    act.wait_ge(s_xms, 2 * (t + 1))
                    act.activation(rs[:, 1, t:t + 1], rs[:, 1, t:t + 1], ACT.Sqrt).then_inc(s_xroot, 1)
                if t >= TT:
                    h2T_out(t - 2)
            act.wait_ge(s_logit, 3)
            act.activation(logitsT[0:NG + NE, :], psL[0:NG + NE, :], ACT.Copy).then_inc(s_logitout, 1)
            act.wait_ge(s_gshift, 1)
            act.activation(gexp, gexp, ACT.Exp).then_inc(s_rexp, 1)
            act.wait_ge(s_diff, 1)
            act.activation(ratio, ratio, ACT.Exp).then_inc(s_rexp, 1)

        @block.vector
        def _(dve):
            dve.tensor_copy(spread_head[0:NH].rearrange("p (h f) -> p h f", f=HD),
                            ident[0:NH, 0:NH].unsqueeze(2).to_broadcast([NH, NH, HD])).then_inc(s_sel, 1)
            dve.tensor_tensor(col[:, 0:KC], k.mod[:, 16:24], k.col(C_P1, KC), ALU.mult).then_inc(s_col, 1)
            dve.scalar_tensor_tensor(col[:, KC:2 * KC], k.mod[:, 32:40], 1.0, k.col(C_G2, KC),
                                     ALU.add, ALU.mult).then_inc(s_col, 1)
            dve.tensor_tensor(col[:, 2 * KC:3 * KC], k.mod[:, 40:48], k.col(C_P2, KC), ALU.mult).then_inc(s_col, 1)
            dve.wait_ge(s_col, 3)
            columns = [col[:, 0:KC], col[:, KC:2 * KC], k.mod[:, 24:32], col[:, 2 * KC:3 * KC]]

            def spread(v):
                for n in range(v * KC, (v + 1) * KC):
                    if n >= 4:
                        dve.wait_ge(s_row, n - 3)
                    dve.tensor_scalar(diag[n % 4], ident, columns[v][:, n % KC:n % KC + 1], None,
                                      ALU.mult).then_inc(s_diag, 1)
                    if n % 4 == 3:
                        dve.wait_ge(s_row, n + 1)
                        half = (n % KC) // 4
                        dve.tensor_copy(rows[v][:, half * 512:(half + 1) * 512], psR[:, :]).then_inc(s_rowout, 1)

            dve.wait_ge(s_oss, 1)
            dve.tensor_scalar(inv, psN[:, 0:TT * NH].rearrange("p (t h) -> p t h", h=NH), 1.0 / HD, EPS,
                              ALU.mult, ALU.add).then_inc(s_oinv, 1)
            dve.wait_ge(s_oinv, 1)
            dve.reciprocal(inv, inv).then_inc(s_oinv, 1)
            for cc in range(FC):
                dve.wait_ge(s_ospread, cc + 1)
                dve.wait_ge(s_gated, cc + 1)
                dve.tensor_tensor(mixT[:, cc, :], mixT[:, cc, :], psO[cc][:, :], ALU.mult).then_inc(s_normed, 1)
            spread(0)
            gt1, a2, b2, _ = rows
            dve.wait_ge(s_rowout, 2)
            dve.wait_ge(s_x1in, 16)
            for t in range(TT):
                dve.wait_ge(s_ysq, 2 * t + 2)
                dve.tensor_tensor(rs[:, 0, t:t + 1], ss[:, 0, t:t + 1], ss[:, 1, t:t + 1], ALU.add).then_inc(s_yms, 1)
                dve.wait_ge(s_yms, 3 * t + 1)
                dve.tensor_scalar(rs[:, 0, t:t + 1], rs[:, 0, t:t + 1], 1.0 / D, EPS, ALU.mult, ALU.add).then_inc(s_yms, 1)
                dve.wait_ge(s_yms, 3 * t + 2)
                dve.reciprocal(rs[:, 0, t:t + 1], rs[:, 0, t:t + 1]).then_inc(s_yms, 1)
                dve.wait_ge(s_yroot, t + 1)
                for i in range(2):
                    c = slice(i * 512, (i + 1) * 512)
                    dve.scalar_tensor_tensor(h2[:, t, c], psY[t % 2][i][:, :], rs[:, 0, t:t + 1], gt1[:, c],
                                             ALU.mult, ALU.mult).then_inc(s_yout, 1)
                dve.wait_ge(s_yout, 2 * t + 2)
                dve.tensor_tensor(x1[:, t, :], x1[:, t, :], h2[:, t, :], ALU.add).then_inc(s_x1, 1)
                dve.wait_ge(s_xsq, t + 1)
                dve.tensor_scalar(rs[:, 1, t:t + 1], ss2[:, t:t + 1], 1.0 / D, EPS, ALU.mult, ALU.add).then_inc(s_xms, 1)
                dve.wait_ge(s_xms, 2 * t + 1)
                dve.reciprocal(rs[:, 1, t:t + 1], rs[:, 1, t:t + 1]).then_inc(s_xms, 1)
                if t == 0:
                    spread(1)
                    spread(2)
                    dve.wait_ge(s_rowout, 6)
                dve.wait_ge(s_xroot, t + 1)
                dve.scalar_tensor_tensor(h2[:, t, :], x1[:, t, :], rs[:, 1, t:t + 1], a2, ALU.mult,
                                         ALU.mult).then_inc(s_h2, 1)
                dve.wait_ge(s_h2, 2 * t + 1)
                dve.tensor_tensor(h2[:, t, :], h2[:, t, :], b2, ALU.add).then_inc(s_h2, 1)
                if t == 0:
                    spread(3)

            dve.tensor_tensor(numbered, ident, k.const("slots")[:, 0:P], ALU.mult).then_inc(s_index, 1)
            dve.memset(summed[:, 0, :], 1.0).then_inc(s_index, 1)
            dve.wait_ge(s_index, 2)
            dve.tensor_reduce(index, numbered, AX.X, ALU.add).then_inc(s_index, 1)
            dve.wait_ge(s_index, 3)

            n = 0

            def made(ins):
                nonlocal n
                n += 1
                ins.then_inc(s_r, 1)

            def done(ins):
                made(ins)
                dve.wait_ge(s_r, n)

            def bc(ap, shape):
                return ap.unsqueeze(2).to_broadcast(shape)

            dve.wait_ge(s_logitp, 1)
            done(dve.tensor_tensor(logits, psR[:, 0:TT * 64].rearrange("p (t j) -> p t j", j=64)[:, :, 0:NG + NE],
                                   k.col(C_RB, NG + NE).unsqueeze(1).to_broadcast([P, TT, NG + NE]), ALU.add))
            groups = logits[:, :, 0:NG]
            experts = logits[:, :, NG:NG + NE].rearrange("p t (g e) -> p t g e", e=EG)
            done(dve.tensor_scalar(first, k.const("experts")[:, 0:EG], -1.0, float(EG), ALU.mult, ALU.add))
            done(dve.tensor_reduce(gmax, groups, AX.X, ALU.max))
            dve.tensor_tensor(gexp, groups, bc(gmax, [P, TT, NG]), ALU.subtract).then_inc(s_gshift, 1)

            def argmax(one_hot, values, largest, eq, best, width):
                done(dve.tensor_tensor(eq, values, bc(largest, [P, TT, width]), ALU.is_equal))
                done(dve.tensor_tensor(eq, eq, first[:, 0:width].unsqueeze(1).to_broadcast([P, TT, width]), ALU.mult))
                done(dve.tensor_reduce(best, eq, AX.X, ALU.max))
                done(dve.tensor_tensor(one_hot, eq, bc(best, [P, TT, width]), ALU.is_equal))

            argmax(gone, groups, gmax, geq, gbest, NG)
            done(dve.tensor_tensor(per_group, experts, gone.unsqueeze(3).to_broadcast([P, TT, NG, EG]), ALU.mult))
            done(dve.tensor_reduce(ing, per_group.rearrange("p t g e -> p t e g"), AX.X, ALU.add))
            for i in range(2):
                done(dve.tensor_reduce(top[i], ing, AX.X, ALU.max))
                argmax(one[i], ing, top[i], eq, best, EG)
                done(dve.tensor_tensor(chosen[i].rearrange("p t (g e) -> p t g e", e=EG),
                                       gone.unsqueeze(3).to_broadcast([P, TT, NG, EG]),
                                       one[i].unsqueeze(2).to_broadcast([P, TT, NG, EG]), ALU.mult))
                if i == 0:
                    done(dve.scalar_tensor_tensor(ing, one[0], NEG, ing, ALU.mult, ALU.add))
            dve.tensor_tensor(ratio, top[1], top[0], ALU.subtract).then_inc(s_diff, 1)
            done(dve.tensor_tensor(both, chosen[0], chosen[1], ALU.add))
            dve.tensor_reduce(both_sum, both.rearrange("p t e -> p e t"), AX.X, ALU.add).then_inc(s_both, 1)
            dve.wait_ge(s_rank, 2)
            dve.tensor_copy(rank[:, 0, :], psT[0][:, 0:NE]).then_inc(s_rankout, 1)
            done(dve.tensor_copy(count, psT[1][:, 0:NE]))
            done(dve.tensor_tensor(over, count.unsqueeze(2).to_broadcast([P, NE, T // SL - 1]),
                                   k.const("tiles").unsqueeze(1).to_broadcast([P, NE, T // SL - 1]), ALU.is_gt))
            done(dve.tensor_reduce(tiles, over, AX.X, ALU.add))
            done(dve.tensor_scalar(tiles, tiles, 1.0, None, ALU.add))
            tiles_upto, tokens_upto = cum[:, 0, :], cum[:, 1, :]
            made(dve.tensor_tensor_scan(tokens_upto, k.const("ones")[:, 0:NE], count, 0.0, ALU.mult, ALU.add))
            done(dve.tensor_tensor_scan(tiles_upto, k.const("ones")[:, 0:NE], tiles, 0.0, ALU.mult, ALU.add))
            done(dve.tensor_scalar(past, tiles_upto, index, None, ALU.is_le))
            done(dve.tensor_tensor(spare, summed, past.unsqueeze(1).to_broadcast([P, 3, NE]), ALU.mult))
            done(dve.tensor_reduce(past_sums, spare, AX.X, ALU.add))
            done(dve.tensor_tensor(item[:, 1:2], index, past_sums[:, 1:2], ALU.subtract))
            dve.tensor_scalar(item[:, 0:1], past_sums[:, 0:1], float(NE - 1), None, ALU.min).then_inc(s_item, 1)
            dve.tensor_scalar(item[:, 1:2], item[:, 1:2], float(SL), float(T - SL), ALU.mult,
                              ALU.min).then_inc(s_item, 1)
            dve.wait_ge(s_item, 2)
            dve.tensor_tensor(item[:, 2:3], past_sums[:, 2:3], item[:, 1:2], ALU.add).then_inc(s_item, 1)
            made(dve.tensor_copy(k.upto, tiles_upto))
            made(dve.tensor_copy(k.tiles, tiles))
            made(dve.tensor_tensor(before, tokens_upto, count, ALU.subtract))
            dve.wait_ge(s_itemrow, 1)
            done(dve.tensor_copy(items[0:1], psL[0:1, 0:3 * 64].rearrange("p (i w) -> p i w", w=64)[
                :, :, 0:ITEMS_MAX + 1]))

    def rows_and_weights(dve, counter):
        n = 0

        def done(ins):
            nonlocal n
            n += 1
            ins.then_inc(counter, 1)
            dve.wait_ge(counter, n)

        done(dve.tensor_tensor(rank, rank, before.unsqueeze(1).to_broadcast([P, TT, NE]), ALU.add))
        for i in range(2):
            done(dve.tensor_tensor(chosen[i], chosen[i], rank, ALU.mult))
            done(dve.tensor_reduce(best, chosen[i], AX.X, ALU.add))
            done(dve.tensor_copy(k.row[i], best))
        done(dve.tensor_reduce(gsum, gexp, AX.X, ALU.add))
        done(dve.tensor_scalar(denom, ratio, 1.0, None, ALU.add))
        done(dve.tensor_tensor(denom, denom, gsum, ALU.mult))
        done(dve.reciprocal(k.weight[0], denom))
        done(dve.tensor_tensor(k.weight[1], k.weight[0], ratio, ALU.mult))

    k.rows_and_weights = rows_and_weights


E_SEL = M_NA + SLOT
E_X = E_SEL + TT * SL
E_SILU = E_X + 512
assert E_SILU + DE // 2 <= M_GT2
E_XT = M_C + CONST["fold"][0]
E_HE = E_XT + 512
assert E_HE + DE // 2 <= M_C + CONST["slots"][0]


def experts(k):
    nc, dram = k.nc, k.dram
    h2 = k.view(M_H2, TT, D)
    sel = k.view(E_SEL, TT, SL)
    x, silu, he = k.view(E_X, 512), k.view(E_SILU, DE // 2), k.view(E_HE, DE // 2)
    y = k.misc(512)
    xT = k.view(E_XT, 4, 2, SL)
    heT = k.misc(2, 2, SL)
    gate_up = [k.view(at, 2, KC, DE) for at in GATE_UP_AT]
    down = [k.view(at, DE // P, D) for at in DOWN_AT]
    ROUNDS = NE // BUFFERS
    ident = k.const("ident")
    psX, psXT, psGU, psHT, psY = k.banks[0:5]

    s_sel, s_x, s_xout = k.sem("s_sel"), k.sem("s_x"), k.sem("s_xout")
    s_xT, s_xTout = k.sem("s_xT"), k.sem("s_xTout")
    s_gu, s_silu, s_he = k.sem("s_gu"), k.sem("s_silu"), k.sem("s_he")
    s_heT, s_heTout = k.sem("s_heT"), k.sem("s_heTout")
    s_down, s_yout, s_store = k.sem("s_down"), k.sem("s_yout"), k.sem("s_store")
    s_end = k.sem("s_end")
    s_router = k.sem("s_router")

    def tiles_of_all(eng):
        return eng.value_load(k.total[0:1, 0:1], min_val=NE, max_val=ITEMS_MAX)

    with nc.Block() as block:
        @block.sync
        def _(sp):
            load_expert(sp, k, 2, 2, parts=(0, 1))

            def load_after(e, j):
                before = sp.value_load(k.upto[0:1, bass.ds(e - BUFFERS, 1)], min_val=1, max_val=ITEMS_MAX)
                sp.wait_ge(s_gu, before)
                load_expert(sp, k, e, j, static=False, parts=(0, 1))
                sp.wait_ge(s_down, before + START)
                load_expert(sp, k, e, j, static=False, parts=(2,))

            with sp.Fori(0, ROUNDS - 1) as it:
                for j in range(BUFFERS):
                    load_after(it * BUFFERS + (j + BUFFERS), j)
            for e in range(ROUNDS * BUFFERS, NE):
                load_after(e, e % BUFFERS)

        @block.tensor
        def _(pe):
            pe.sem_inc(s_down, START)
            pe.sem_inc(s_heT, START)
            def gather(part):
                for t in range(part * TT // 2, (part + 1) * TT // 2):
                    for half in range(2):
                        mm = pe.matmul(psX[half * SL:(half + 1) * SL, :], sel[:, t, :],
                                       h2[:, t, half * 512:(half + 1) * 512], start=(t == 0), stop=(t == TT - 1))
                if part == 1:
                    mm.then_inc(s_x, 1)

            def transpose_x():
                for c in range(4):
                    mm = pe.transpose(psXT[:, c * P:(c + 1) * P], x[:, c * P:(c + 1) * P], ident)
                mm.then_inc(s_xT, 1)

            def tile(w, it, j):
                gate_there, up_there, down_there = k.s_expert[j]
                pe.wait_ge(gate_there, it * 16 + 16)
                pe.wait_ge(up_there, it * 16 + 16)
                pe.wait_ge(s_xTout, w + 1)
                for c in range(KC):
                    for half in range(2):
                        mm = pe.matmul(psGU[half * SL:(half + 1) * SL, :], xT[:, c % 4, c // 4, :],
                                       gate_up[j][:, :, c, half * (DE // 2):(half + 1) * (DE // 2)],
                                       start=(c == 0), stop=(c == KC - 1))
                mm.then_inc(s_gu, 1)
                pe.wait_ge(s_sel, w + 2)
                gather(0)
                pe.wait_ge(s_he, w + 1 + START)
                for c in range(2):
                    mm = pe.transpose(psHT[:, c * P:(c + 1) * P], he[:, c * P:(c + 1) * P], ident)
                mm.then_inc(s_heT, 1)
                gather(1)
                pe.wait_ge(down_there, it * 16 + 16)
                pe.wait_ge(s_heTout, w + 1)
                pe.wait_ge(s_yout, w + START)
                for c in range(DE // P):
                    if c == DE // P // 2:
                        pe.wait_ge(s_xout, w + 2)
                        transpose_x()
                    for half in range(2):
                        mm = pe.matmul(psY[half * SL:(half + 1) * SL, :], heT[:, c % 2, c // 2, :],
                                       down[j][:, c, half * 512:(half + 1) * 512],
                                       start=(c == 0), stop=(c == DE // P - 1))
                mm.then_inc(s_down, 1)

            pe.wait_ge(s_sel, 1)
            gather(0)
            gather(1)
            pe.wait_ge(s_xout, 1)
            transpose_x()
            done = pe.alloc_register("tiles_done")
            pe.reg_mov(done, 0)

            def expert(e, it, j):
                tiles = pe.value_load(k.tiles[0:1, bass.ds(e, 1)], min_val=1, max_val=T // SL)
                with pe.Fori(0, tiles) as _t:
                    tile(pe.snap(done, min_val=0, max_val=ITEMS_MAX), it, j)
                    pe.reg_add(done, done, 1)

            with pe.Fori(0, ROUNDS) as it:
                for j in range(BUFFERS):
                    expert(it * BUFFERS + j, it, j)
            for e in range(ROUNDS * BUFFERS, NE):
                expert(e, ROUNDS, e % BUFFERS)

        @block.scalar
        def _(act):
            act.sem_inc(s_store, START)
            total = tiles_of_all(act)
            act.wait_ge(s_x, 1)
            act.activation(x, psX[:, :], ACT.Copy).then_inc(s_xout, 1)
            with act.Fori(0, total) as w:
                row = act.value_load(k.item_row[0:1, bass.ds(w, 1)], min_val=0, max_val=ROWS_OUT)
                act.wait_ge(s_gu, w + 1)
                act.wait_ge(s_he, w + START)
                act.activation(silu, psGU[:, 0:DE // 2], ACT.Silu).then_inc(s_silu, 1)
                act.wait_ge(s_heT, w + 1 + START)
                act.wait_ge(s_down, w + START)
                act.activation(heT.rearrange("p a b c -> p (a b c)"), psHT[:, 0:2 * P], ACT.Copy).then_inc(s_heTout, 1)
                act.wait_ge(s_x, w + 2)
                act.wait_ge(s_xT, w + 1)
                act.activation(x, psX[:, :], ACT.Copy).then_inc(s_xout, 1)
                act.wait_ge(s_yout, w + 1 + START)
                act.dma_start(dram["rows"][bass.ds(row, SL), :].rearrange("r (h n) -> h r n", h=2),
                              y).then_inc(s_store, 16)
            act.wait_ge(s_store, total * 16 + START)
            act.sem_inc(s_end, 1)

        @block.vector
        def _(dve):
            dve.sem_inc(s_he, START)
            dve.sem_inc(s_yout, START)
            def select(w):
                e = dve.value_load(k.item_e[0:1, bass.ds(w, 1)], min_val=0, max_val=NE - 1)
                t = dve.value_load(k.item_place[0:1, bass.ds(w, 1)], min_val=0, max_val=T - SL)
                return (k.const("slots")[:, bass.ds(t, SL)].unsqueeze(1).to_broadcast([P, TT, SL]),
                        k.place[:, :, bass.ds(e, 1)].to_broadcast([P, TT, SL]))

            total = tiles_of_all(dve)
            places, place = select(0)
            dve.tensor_tensor(sel, places, place, ALU.is_equal).then_inc(s_sel, 1)
            dve.wait_ge(s_xT, 1)
            dve.tensor_copy(xT.rearrange("p a b c -> p (a b c)"), psXT[:, :]).then_inc(s_xTout, 1)
            k.rows_and_weights(dve, s_router)
            with dve.Fori(0, total) as w:
                places, place = select(w + 1)
                dve.wait_ge(s_x, w + 1)
                dve.tensor_tensor(sel, places, place, ALU.is_equal).then_inc(s_sel, 1)
                dve.wait_ge(s_silu, w + 1)
                dve.wait_ge(s_heT, w + START)
                dve.tensor_tensor(he, silu, psGU[:, DE // 2:DE], ALU.mult).then_inc(s_he, 1)
                dve.wait_ge(s_xT, w + 2)
                dve.wait_ge(s_gu, w + 1)
                dve.tensor_copy(xT.rearrange("p a b c -> p (a b c)"), psXT[:, :]).then_inc(s_xTout, 1)
                dve.wait_ge(s_down, w + 1 + START)
                dve.wait_ge(s_store, w * 16 + START)
                dve.tensor_copy(y, psY[:, :]).then_inc(s_yout, 1)


def finish(k):
    nc, dram = k.nc, k.dram
    x1 = k.view(M_X1, TT, D)
    gt2 = k.view(M_GT2, D)
    picked = k.view(0, 2, TT, D)
    total = k.view(2 * TT * D, TT, D)
    junk = k.view(3 * TT * D, D)
    ms, rstd = k.misc(TT), k.misc(TT)
    s_gather = [k.sem(f"s_gather{t}") for t in range(TT)]
    s_first = k.sem("s_first")
    s_sum = k.sem("s_sum")
    s_scaled = k.sem("s_scaled")
    s_last = k.sem("s_last")
    s_sq = k.sem("s_sq")
    s_ms = k.sem("s_ms")
    s_root = k.sem("s_root")
    s_out = k.sem("s_out")
    s_stored = k.sem("s_stored")

    with nc.Block() as block:
        @block.gpsimd
        def _(pool):
            for t in range(TT):
                for i in range(2):
                    pool.indirect_dma_start(picked[:, i, t, :], None, dram["rows"][0:ROWS_OUT, :],
                                            bass.IndirectOffsetOnAxis(ap=k.row[i][:, t:t + 1], axis=0)
                                            ).then_inc(s_gather[t], 16)
            for t in range(TT - 1):
                pool.wait_ge(s_scaled, t + 1)
                pool.tensor_tensor(total[:, t, :], total[:, t, :], x1[:, t, :], ALU.add).then_inc(s_out, 1)

        @block.vector
        def _(dve):
            for t in range(TT + 1):
                if t < TT:
                    dve.wait_ge(s_first, t + 1)
                    dve.scalar_tensor_tensor(total[:, t, :], picked[:, 1, t, :], k.weight[1][:, t:t + 1],
                                             total[:, t, :], ALU.mult, ALU.add).then_inc(s_sum, 1)
                if t >= 1:
                    v = t - 1
                    dve.wait_ge(s_sq, v + 1)
                    dve.tensor_scalar(rstd[:, v:v + 1], ms[:, v:v + 1], 1.0 / D, EPS, ALU.mult, ALU.add).then_inc(s_ms, 1)
                    dve.wait_ge(s_ms, 2 * v + 1)
                    dve.reciprocal(rstd[:, v:v + 1], rstd[:, v:v + 1]).then_inc(s_ms, 1)
                    dve.wait_ge(s_root, v + 1)
                    dve.scalar_tensor_tensor(total[:, v, :], total[:, v, :], rstd[:, v:v + 1], gt2, ALU.mult,
                                             ALU.mult).then_inc(s_scaled, 1)
                    if v == TT - 1:
                        dve.wait_ge(s_scaled, v + 1)
                        dve.tensor_tensor(total[:, v, :], total[:, v, :], x1[:, v, :], ALU.add).then_inc(s_last, 1)

        @block.scalar
        def _(act):
            for t in range(TT + 1):
                if t < TT:
                    act.wait_ge(s_gather[t], 32)
                    act.activation(total[:, t, :], picked[:, 0, t, :], ACT.Copy,
                                   scale=k.weight[0][:, t:t + 1]).then_inc(s_first, 1)
                if t >= 1:
                    v = t - 1
                    act.wait_ge(s_sum, v + 1)
                    if v:
                        act.wait_ge(s_sq, v)
                    act.activation(junk, total[:, v, :], ACT.Square, accum_out=ms[:, v:v + 1]).then_inc(s_sq, 1)
                    act.wait_ge(s_ms, 2 * v + 2)
                    act.activation(rstd[:, v:v + 1], rstd[:, v:v + 1], ACT.Sqrt).then_inc(s_root, 1)

        @block.sync
        def _(sp):
            for t in range(TT):
                if t < TT - 1:
                    sp.wait_ge(s_out, t + 1)
                else:
                    sp.wait_ge(s_last, 1)
                sp.dma_start(dram["out"][t * P:(t + 1) * P, :], total[:, t, :]).then_inc(s_stored, 16)
            sp.wait_ge(s_stored, 16 * TT)


def layout(i):
    a = {n: np.asarray(v) for n, v in i.items()}

    def cols(v):
        return v.reshape(-1, P).T

    def rows(v):
        return np.broadcast_to(v[None, :], (P, v.size))

    w_conv = a["w_conv_dn"][0]
    parts = [cols(a["b_ada"][0]), cols(a["g_pre_mix"][0]), cols(a["g_post_mix"][0]), cols(a["g_pre_ffn"][0]),
             cols(a["g_post_ffn"][0]), cols(a["c"][0]),
             w_conv.reshape(CONV, 3 * FC, P).transpose(2, 1, 0).reshape(P, -1),
             np.concatenate([a["g_onorm_dn"][0]] * 2)[:, None],
             np.repeat(a["a_log_dn"][0], CH, axis=0), np.repeat(a["dt_bias_dn"][0], CH, axis=0),
             rows(a["b_group"][0]), rows(a["b_expert"][0])]
    rpb = np.pad(a["rpb_na"][0], ((0, 0), (0, 0), (16, 17)))
    r, c = np.divmod(np.arange(P), WIN)
    bias = rpb[:, (7 - r)[:, None, None] + np.arange(ROWS)[None, :, None],
               (15 - c)[:, None, None] + np.arange(QB)[None, None, :]].transpose(1, 0, 2, 3)
    cs = constants()
    return {
        "x": a["x"][0], "cols": np.concatenate(parts, axis=1), "consts": np.concatenate([cs[n] for n in CONST], axis=1),
        "w_ada": a["w_ada"][0], "w_in": a["w_in"][0], "w_out": a["w_out"][0], "bias": bias.reshape(P, -1),
        "w_route": np.concatenate([a["w_group"][0], a["w_expert"][0]], axis=1),
        "w_gate": a["w_gate"][0], "w_up": a["w_up"][0], "w_down": a["w_down"][0],
    }


STAGES = [project, attend, delta, route, experts, finish]


def build(nc, dram, stages):
    with ExitStack() as ctx:
        k = Kernel(nc, ctx, dram)

        def run(stage):
            k.stage = stage.__name__
            stage(k)
            k.end_stage()

        with nc.sbuf_tensor("parts", [P, SPLIT], F32R) as parts:
            k.parts = parts[:, :]
            run(stages[0])
        k.lower = ctx.enter_context(nc.sbuf_tensor("lower", [P, SPLIT], F32))
        for stage in stages[1:]:
            run(stage)


def kernel(**inputs):
    import concourse.bacc as bacc
    from concourse.bass_utils import run_bass_kernel_spmd

    nc = bacc.Bacc("TRN2", target_bir_lowering=False, num_devices=1)
    arrays = {n: np.ascontiguousarray(v) for n, v in layout(inputs).items()}
    dram = {n: nc.dram_tensor(f"in_{n}", v.shape, mybir.dt.from_np(v.dtype), kind="ExternalInput").ap()
            for n, v in arrays.items()}
    dram["out"] = nc.dram_tensor("out", (T, D), F32, kind="ExternalOutput").ap()
    dram["rows"] = nc.dram_tensor("rows", (ROWS_OUT + SL, D), F32, kind="Internal").ap()
    build(nc, dram, STAGES)
    r = run_bass_kernel_spmd(nc, [{f"in_{n}": v for n, v in arrays.items()}], core_ids=[0])
    return r.results[0]["out"].reshape(1, T, D)
```
